# Optimizing a Trainium2 kernel written in Bass

```python
import jax, jax.numpy as jnp
from jax import lax
import numpy as np
import math
import jax
import jax.numpy as jnp

D_MODEL = 1024
BATCH = 1
SEQ = 256
DEPTH = 2

CHUNK = 64
N_EVEN = (DEPTH + 1) // 2
N_ODD = DEPTH // 2
EPS = 1e-6
ROPE_THETA = 10000.0

GM_GROUPS = 4
GM_GROUP_DIM = 128
GM_WIDTH = GM_GROUPS * GM_GROUP_DIM
GM_BLOCK = 128
MLA_HEADS = 8
MLA_Q_RANK = 384
MLA_KV_RANK = 256
MLA_NOPE = 64
MLA_ROPE = 32
MLA_V = 64
MLA_QK = MLA_NOPE + MLA_ROPE
ATTN_BLOCK = 128
EVEN_IN = 2 * GM_WIDTH + MLA_Q_RANK + MLA_KV_RANK + MLA_ROPE
EVEN_MIX = GM_WIDTH + MLA_HEADS * MLA_V
RET_HEADS = 4
RET_QK = 256
RET_V = 512
ODD_IN = 2 * RET_HEADS * RET_QK + 2 * RET_HEADS * RET_V
ODD_MIX = RET_HEADS * RET_V
D_FF = -(-8 * D_MODEL // (3 * 256)) * 256


def rmsnorm(x, g):
    xf = x.astype(jnp.float32)
    y = xf * lax.rsqrt(jnp.mean(xf * xf, axis=-1, keepdims=True) + EPS)
    return (y * g.astype(jnp.float32)).astype(x.dtype)

def rope(x, pos):
    half = x.shape[-1] // 2
    inv = ROPE_THETA ** (-jnp.arange(half, dtype=jnp.float32) / half)
    ang = pos.astype(jnp.float32)[:, None] * inv[None, :]
    cos = jnp.cos(ang)[None, :, None, :]
    sin = jnp.sin(ang)[None, :, None, :]
    xf = x.astype(jnp.float32)
    x1, x2 = xf[..., :half], xf[..., half:]
    return jnp.concatenate([x1 * cos - x2 * sin, x2 * cos + x1 * sin], axis=-1).astype(x.dtype)

def spatial_gating(u, v, v_norm, w_s, b_s):
    B, S, _ = u.shape
    n = S // GM_BLOCK
    v = rmsnorm(v.reshape(B, S, GM_GROUPS, GM_GROUP_DIM), v_norm)
    cid = jnp.arange(GM_BLOCK) // CHUNK
    w = jnp.where((cid[None, :] <= cid[:, None])[None], w_s, 0)
    vb = v.reshape(B, n, GM_BLOCK, GM_GROUPS, GM_GROUP_DIM)
    s = jnp.einsum('gts,bnsgc->bntgc', w, vb) + b_s.T[:, :, None]
    ub = u.reshape(B, n, GM_BLOCK, GM_GROUPS, GM_GROUP_DIM)
    return (ub * s).reshape(B, S, GM_WIDTH)

def block_causal_attention(q, k, v):
    S = q.shape[1]
    scale = MLA_QK ** -0.5
    chunk_id = jnp.arange(S) // CHUNK
    outs = []
    for start in range(0, S, ATTN_BLOCK):
        end = start + ATTN_BLOCK
        s = jnp.einsum('bqhd,bkhd->bhqk', q[:, start:end], k[:, :end]).astype(jnp.float32) * scale
        mask = chunk_id[None, :end] <= chunk_id[start:end, None]
        p = jax.nn.softmax(jnp.where(mask, s, -jnp.inf), axis=-1).astype(v.dtype)
        outs.append(jnp.einsum('bhqk,bkhd->bqhd', p, v[:, :end]))
    return jnp.concatenate(outs, axis=1)

def mla(c_q, c_kv, k_pe, q_a_norm, w_uq, kv_a_norm, w_ukv, q_norm, k_norm, pos):
    B, S, _ = c_q.shape
    q = (rmsnorm(c_q, q_a_norm) @ w_uq).reshape(B, S, MLA_HEADS, MLA_QK)
    kv = (rmsnorm(c_kv, kv_a_norm) @ w_ukv).reshape(B, S, MLA_HEADS, MLA_NOPE + MLA_V)
    k = jnp.concatenate([kv[..., :MLA_NOPE],
                         jnp.broadcast_to(k_pe[:, :, None, :], (B, S, MLA_HEADS, MLA_ROPE))], axis=-1)
    v = kv[..., MLA_NOPE:]
    q = rmsnorm(q, q_norm)
    k = rmsnorm(k, k_norm)
    q = jnp.concatenate([q[..., :MLA_NOPE], rope(q[..., MLA_NOPE:], pos)], axis=-1)
    k = jnp.concatenate([k[..., :MLA_NOPE], rope(k[..., MLA_NOPE:], pos)], axis=-1)
    o = block_causal_attention(q, k, v)
    return o.reshape(B, S, MLA_HEADS * MLA_V)

def even_mixer(h, w_in, gm_v_norm, gm_w_s, gm_b_s, q_a_norm, w_uq, kv_a_norm, w_ukv,
               q_norm, k_norm, w_out, pos):
    z = h @ w_in
    o1 = GM_WIDTH
    o2 = 2 * GM_WIDTH
    o3 = o2 + MLA_Q_RANK
    o4 = o3 + MLA_KV_RANK
    u = jax.nn.gelu(z[..., :o1])
    v = jax.nn.gelu(z[..., o1:o2])
    a = spatial_gating(u, v, gm_v_norm, gm_w_s, gm_b_s)
    b = mla(z[..., o2:o3], z[..., o3:o4], z[..., o4:], q_a_norm, w_uq, kv_a_norm, w_ukv,
            q_norm, k_norm, pos)
    return jnp.concatenate([a, b], axis=-1) @ w_out

def retention(q, k, v):
    B, S, H, dk = q.shape
    dv = v.shape[-1]
    n = S // CHUNK
    lg = jnp.log(1.0 - 2.0 ** (-5.0 - jnp.arange(H, dtype=jnp.float32)))
    j = jnp.arange(CHUNK, dtype=jnp.float32)
    diff = j[:, None] - j[None, :]
    dmask = jnp.where(diff >= 0, jnp.exp(lg[:, None, None] * jnp.maximum(diff, 0.0)), 0.0)
    xi = jnp.exp(lg[:, None] * (j + 1.0))[None, :, :, None]
    zeta = jnp.exp(lg[:, None] * (CHUNK - 1.0 - j))[None, :, :, None]
    g_chunk = jnp.exp(lg * CHUNK)[None, :, None, None]

    def to_chunks(t):
        return t.astype(jnp.float32).reshape(B, n, CHUNK, H, -1).transpose(1, 0, 3, 2, 4)

    qc = to_chunks(q)
    kc = to_chunks(k) * (dk ** -0.5)
    vc = to_chunks(v)

    def step(state, inp):
        qi, ki, vi = inp
        a = jnp.einsum('bhjd,bhmd->bhjm', qi, ki) * dmask
        o = jnp.einsum('bhjm,bhme->bhje', a, vi) + jnp.einsum('bhjd,bhde->bhje', qi, state) * xi
        state = state * g_chunk + jnp.einsum('bhmd,bhme->bhde', ki * zeta, vi)
        return state, o

    state0 = jnp.zeros((B, H, dk, dv), jnp.float32)
    _, o = lax.scan(step, state0, (qc, kc, vc))
    return o.transpose(1, 0, 3, 2, 4).reshape(B, S, H, dv)

def odd_mixer(h, w_in, out_norm, w_out, pos):
    B, S, _ = h.shape
    nq = RET_HEADS * RET_QK
    nv = RET_HEADS * RET_V
    z = h @ w_in
    q = rope(z[..., :nq].reshape(B, S, RET_HEADS, RET_QK), pos)
    k = rope(z[..., nq:2 * nq].reshape(B, S, RET_HEADS, RET_QK), pos)
    v = z[..., 2 * nq:2 * nq + nv].reshape(B, S, RET_HEADS, RET_V)
    g = z[..., 2 * nq + nv:]
    o = rmsnorm(retention(q, k, v), out_norm)
    o = o.reshape(B, S, nv).astype(h.dtype) * jax.nn.silu(g)
    return o @ w_out

def swiglu(h, w_gate, w_up, w_down):
    return (jax.nn.silu(h @ w_gate) * (h @ w_up)) @ w_down

def first_inputs(seed: int = 0) -> dict:
    key = jax.random.key(seed)
    ks = jax.random.split(key, 24)
    f32 = jnp.float32

    def w(k, shape, fan_in):
        return jax.random.normal(k, shape, f32) * (fan_in ** -0.5)

    def gain(k, shape):
        return 1.0 + 0.1 * jax.random.normal(k, shape, f32)

    return {
        "x": jax.random.normal(ks[0], (BATCH, SEQ, D_MODEL), f32),
        "norm_mix": gain(ks[1], (DEPTH, D_MODEL)),
        "norm_ffn": gain(ks[2], (DEPTH, D_MODEL)),
        "even_w_in": w(ks[3], (N_EVEN, D_MODEL, EVEN_IN), D_MODEL),
        "gm_v_norm": gain(ks[4], (N_EVEN, GM_GROUPS, GM_GROUP_DIM)),
        "gm_w_s": w(ks[5], (N_EVEN, GM_GROUPS, GM_BLOCK, GM_BLOCK), GM_BLOCK),
        "gm_b_s": gain(ks[6], (N_EVEN, GM_GROUPS, GM_BLOCK)),
        "mla_q_a_norm": gain(ks[7], (N_EVEN, MLA_Q_RANK)),
        "mla_w_uq": w(ks[8], (N_EVEN, MLA_Q_RANK, MLA_HEADS * MLA_QK), MLA_Q_RANK),
        "mla_kv_a_norm": gain(ks[9], (N_EVEN, MLA_KV_RANK)),
        "mla_w_ukv": w(ks[10], (N_EVEN, MLA_KV_RANK, MLA_HEADS * (MLA_NOPE + MLA_V)), MLA_KV_RANK),
        "mla_q_norm": gain(ks[11], (N_EVEN, MLA_QK)),
        "mla_k_norm": gain(ks[12], (N_EVEN, MLA_QK)),
        "even_w_out": w(ks[13], (N_EVEN, EVEN_MIX, D_MODEL), EVEN_MIX),
        "odd_w_in": w(ks[14], (N_ODD, D_MODEL, ODD_IN), D_MODEL),
        "ret_out_norm": gain(ks[15], (N_ODD, RET_HEADS, RET_V)),
        "odd_w_out": w(ks[16], (N_ODD, ODD_MIX, D_MODEL), ODD_MIX),
        "ffn_w_gate": w(ks[17], (DEPTH, D_MODEL, D_FF), D_MODEL),
        "ffn_w_up": w(ks[18], (DEPTH, D_MODEL, D_FF), D_MODEL),
        "ffn_w_down": w(ks[19], (DEPTH, D_FF, D_MODEL), D_FF),
    }

def first_block(x, norm_mix, norm_ffn, even_w_in, gm_v_norm, gm_w_s, gm_b_s,
              mla_q_a_norm, mla_w_uq, mla_kv_a_norm, mla_w_ukv, mla_q_norm, mla_k_norm,
              even_w_out, odd_w_in, ret_out_norm, odd_w_out,
              ffn_w_gate, ffn_w_up, ffn_w_down):
    pos = jnp.arange(x.shape[1])
    for l in range(DEPTH):
        i = l // 2
        h = rmsnorm(x, norm_mix[l])
        if l % 2 == 0:
            mix = even_mixer(h, even_w_in[i], gm_v_norm[i], gm_w_s[i], gm_b_s[i],
                             mla_q_a_norm[i], mla_w_uq[i], mla_kv_a_norm[i], mla_w_ukv[i],
                             mla_q_norm[i], mla_k_norm[i], even_w_out[i], pos)
        else:
            mix = odd_mixer(h, odd_w_in[i], ret_out_norm[i], odd_w_out[i], pos)
        x = x + mix
        h = rmsnorm(x, norm_ffn[l])
        x = x + swiglu(h, ffn_w_gate[l], ffn_w_up[l], ffn_w_down[l])
    return x


D_FF_2 = 4096
LN_EPS = 1e-5
NORM_EPS = 1e-6
H_A = 4
DK_A = 128
DV_A = 128
CONV_K = 4
A_QK = H_A * DK_A
A_V = H_A * DV_A
H_B = 4
D_B = 128
B_PREV = 8
REL_CLIP = 128
B_W = H_B * D_B
H_C = 8
HKV_C = 2
G_C = H_C // HKV_C
D_C = 64
WINDOW = 128
C_PREV = WINDOW // CHUNK
C_Q = H_C * D_C
C_KV = HKV_C * D_C
N_BRANCH = 3
IN_SPLITS = (A_QK, A_QK, A_V, H_A, H_A, A_V, B_W, B_W, B_W, C_Q, C_KV, C_KV)
D_IN = sum(IN_SPLITS)


def layer_norm(x, g, b):
    xf = x.astype(jnp.float32)
    mu = jnp.mean(xf, -1, keepdims=True)
    xc = xf - mu
    var = jnp.mean(xc * xc, -1, keepdims=True)
    return (xc * lax.rsqrt(var + LN_EPS) * g.astype(jnp.float32) + b.astype(jnp.float32)).astype(x.dtype)

def swiglu_2(x, w_in, w_out):
    gate, up = jnp.split(x @ w_in, 2, axis=-1)
    return (jax.nn.silu(gate) * up) @ w_out

def causal_depthwise_conv(x, w):
    k = w.shape[0]
    return lax.conv_general_dilated(x, w[:, None, :], window_strides=(1,), padding=[(k - 1, 0)],
                                    dimension_numbers=('NWC', 'WIO', 'NWC'),
                                    feature_group_count=x.shape[-1])

def l2_normalize(x):
    return x * lax.rsqrt(jnp.sum(x * x, -1, keepdims=True) + NORM_EPS)

def to_chunks(a):
    b, t, h = a.shape[:3]
    a = a.reshape(b, t // CHUNK, CHUNK, h, *a.shape[3:])
    return jnp.moveaxis(a, (1, 3), (0, 2))

def chunk_gated_delta_rule(q, k, v, g, beta):
    b, t, h, dk = q.shape
    dv = v.shape[-1]
    q = to_chunks(q) * (dk ** -0.5)
    k = to_chunks(k)
    v = to_chunks(v)
    g = to_chunks(g)
    beta = to_chunks(beta)
    g_cum = jnp.cumsum(g, axis=-1)
    idx = jnp.arange(CHUNK)
    causal = idx[:, None] >= idx[None, :]
    strict = idx[:, None] > idx[None, :]
    decay = jnp.exp(jnp.where(causal, g_cum[..., :, None] - g_cum[..., None, :], -jnp.inf))
    k_beta = k * beta[..., None]
    lower = jnp.where(strict, jnp.einsum('nbhid,nbhjd->nbhij', k_beta, k) * decay, 0.0)
    eye = jnp.eye(CHUNK, dtype=jnp.float32)
    rhs = jnp.concatenate([v * beta[..., None], k_beta * jnp.exp(g_cum)[..., None]], axis=-1)
    uw = lax.linalg.triangular_solve(eye + lower, rhs, left_side=True, lower=True, unit_diagonal=True)
    u, w = uw[..., :dv], uw[..., dv:]
    attn = jnp.einsum('nbhid,nbhjd->nbhij', q, k) * decay
    q_dec = q * jnp.exp(g_cum)[..., None]
    g_last = g_cum[..., -1]
    k_dec = k * jnp.exp(g_last[..., None] - g_cum)[..., None]

    def step(state, inp):
        q_c, k_c, u_c, w_c, a_c, gl_c = inp
        v_new = u_c - jnp.einsum('bhcd,bhdv->bhcv', w_c, state)
        o_c = jnp.einsum('bhcd,bhdv->bhcv', q_c, state) + jnp.einsum('bhij,bhjv->bhiv', a_c, v_new)
        state = state * jnp.exp(gl_c)[..., None, None] + jnp.einsum('bhcd,bhcv->bhdv', k_c, v_new)
        return state, o_c

    s0 = jnp.zeros((b, h, dk, dv), jnp.float32)
    _, o = lax.scan(step, s0, (q_dec, k_dec, u, w, attn, g_last))
    o = jnp.moveaxis(o, (0, 2), (1, 3))
    return o.reshape(b, t, h, dv)

def gated_deltanet(qa, ka, va, beta_raw, a_raw, za, conv_w, a_log, dt_bias, norm_g):
    b, t, _ = qa.shape
    f32 = jnp.float32
    qkv = jax.nn.silu(causal_depthwise_conv(jnp.concatenate([qa, ka, va], -1), conv_w)).astype(f32)
    q, k, v = jnp.split(qkv, [A_QK, 2 * A_QK], axis=-1)
    q = l2_normalize(q.reshape(b, t, H_A, DK_A))
    k = l2_normalize(k.reshape(b, t, H_A, DK_A))
    v = v.reshape(b, t, H_A, DV_A)
    beta = jax.nn.sigmoid(beta_raw.astype(f32))
    g = -jnp.exp(a_log.astype(f32)) * jax.nn.softplus(a_raw.astype(f32) + dt_bias.astype(f32))
    o = chunk_gated_delta_rule(q, k, v, g, beta)
    z = za.reshape(b, t, H_A, DV_A).astype(f32)
    o = o * lax.rsqrt(jnp.mean(o * o, -1, keepdims=True) + NORM_EPS) * norm_g.astype(f32) * jax.nn.silu(z)
    return o.reshape(b, t, A_V).astype(qa.dtype)

def chunk_band(a, n_prev):
    b, t = a.shape[:2]
    n = t // CHUNK
    pad = [(0, 0), (n_prev * CHUNK, 0)] + [(0, 0)] * (a.ndim - 2)
    ap = jnp.pad(a, pad).reshape(b, n + n_prev, CHUNK, *a.shape[2:])
    band = jnp.stack([ap[:, j:j + n] for j in range(n_prev + 1)], axis=2)
    return band.reshape(b, n, (n_prev + 1) * CHUNK, *a.shape[2:])

def band_geometry(n, n_prev):
    i = jnp.arange(CHUNK)
    j = jnp.arange((n_prev + 1) * CHUNK)
    dist = n_prev * CHUNK + i[:, None] - j[None, :]
    valid = (jnp.arange(n)[:, None] - n_prev + j[None, :] // CHUNK) >= 0
    return dist, valid

def alibi_slopes(n):
    return 2.0 ** (-8.0 * jnp.arange(1, n + 1, dtype=jnp.float32) / n)

def chunk_relpos_attention(q, k, v, rel_bias):
    b, t, _ = q.shape
    n = t // CHUNK
    q = q.reshape(b, n, CHUNK, H_B, D_B)
    kb = chunk_band(k.reshape(b, t, H_B, D_B), B_PREV)
    vb = chunk_band(v.reshape(b, t, H_B, D_B), B_PREV)
    s = jnp.einsum('bnqhd,bnkhd->bnhqk', q, kb).astype(jnp.float32) * (D_B ** -0.5)
    dist, valid = band_geometry(n, B_PREV)
    rel_idx = jnp.clip(dist, -(CHUNK - 1), REL_CLIP) + (CHUNK - 1)
    bias = rel_bias.astype(jnp.float32)[:, rel_idx]
    s = jnp.where(valid[None, :, None, None, :], s + bias, -jnp.inf)
    p = jax.nn.softmax(s, axis=-1).astype(v.dtype)
    o = jnp.einsum('bnhqk,bnkhd->bnqhd', p, vb)
    return o.reshape(b, t, B_W)

def swa_sink_attention(q, k, v, sinks):
    b, t, _ = q.shape
    n = t // CHUNK
    q = q.reshape(b, n, CHUNK, HKV_C, G_C, D_C)
    kb = chunk_band(k.reshape(b, t, HKV_C, D_C), C_PREV)
    vb = chunk_band(v.reshape(b, t, HKV_C, D_C), C_PREV)
    s = jnp.einsum('bnqhgd,bnkhd->bnhgqk', q, kb).astype(jnp.float32) * (D_C ** -0.5)
    dist, valid = band_geometry(n, C_PREV)
    slopes = alibi_slopes(H_C).reshape(HKV_C, G_C)
    s = s - slopes[:, :, None, None] * jnp.abs(dist).astype(jnp.float32)
    s = jnp.where(valid[None, :, None, None, None, :], s, -jnp.inf)
    sink = jnp.broadcast_to(sinks.astype(jnp.float32).reshape(HKV_C, G_C)[:, :, None, None], s.shape[:-1] + (1,))
    p = jax.nn.softmax(jnp.concatenate([s, sink], axis=-1), axis=-1)[..., :-1].astype(v.dtype)
    o = jnp.einsum('bnhgqk,bnkhd->bnqhgd', p, vb)
    return o.reshape(b, t, C_Q)

def hybrid_mixer(x, w_in, b_in, conv_w, a_log, dt_bias, gdn_norm_g, rel_bias, sinks,
                 w_gate, b_gate, w_br_a, w_br_b, w_br_c, w_out):
    b, t, d = x.shape
    proj = x @ w_in + b_in
    split_at = np.cumsum(IN_SPLITS)[:-1].tolist()
    (qa, ka, va, beta_raw, a_raw, za, qb, kb, vb, qc, kc, vc) = jnp.split(proj, split_at, axis=-1)
    o_a = gated_deltanet(qa, ka, va, beta_raw, a_raw, za, conv_w, a_log, dt_bias, gdn_norm_g)
    o_b = chunk_relpos_attention(qb, kb, vb, rel_bias)
    o_c = swa_sink_attention(qc, kc, vc, sinks)
    gates = jax.nn.sigmoid(x @ w_gate + b_gate).reshape(b, t, N_BRANCH, d)
    merged = (gates[:, :, 0] * (o_a @ w_br_a) + gates[:, :, 1] * (o_b @ w_br_b)
              + gates[:, :, 2] * (o_c @ w_br_c))
    return merged @ w_out

def second_inputs(seed: int = 0) -> dict:
    key = jax.random.key(seed)
    keys = list(jax.random.split(key, 32))
    f32 = jnp.float32
    L, D = DEPTH, D_MODEL
    sub_scale = (8.0 * DEPTH) ** -0.25

    def nrm(shape, scale):
        return jax.random.normal(keys.pop(), shape, f32) * scale

    def gain(shape):
        return 1.0 + nrm(shape, 0.02)

    x = nrm((BATCH, SEQ, D), 1.0)
    ln1_g = gain((L, D))
    ln1_b = nrm((L, D), 0.02)
    w_ff1_in = nrm((L, D, 2 * D_FF_2), D ** -0.5)
    w_ff1_out = nrm((L, D_FF_2, D), D_FF_2 ** -0.5 * sub_scale)
    w_in = nrm((L, D, D_IN), D ** -0.5)
    b_in = nrm((L, D_IN), 0.02)
    conv_w = nrm((L, CONV_K, 2 * A_QK + A_V), CONV_K ** -0.5)
    a_log = jnp.log(jax.random.uniform(keys.pop(), (L, H_A), f32, 1.0, 16.0))
    dt = jnp.exp(jax.random.uniform(keys.pop(), (L, H_A), f32, math.log(1e-3), math.log(1e-1)))
    dt_bias = dt + jnp.log(-jnp.expm1(-dt))
    gdn_norm_g = gain((L, DV_A))
    rel_bias = nrm((L, H_B, CHUNK + REL_CLIP), 0.1)
    sinks = nrm((L, H_C), 0.5)
    w_gate = nrm((L, D, N_BRANCH * D), D ** -0.5)
    b_gate = nrm((L, N_BRANCH * D), 0.02)
    w_br_a = nrm((L, A_V, D), A_V ** -0.5 * sub_scale)
    w_br_b = nrm((L, B_W, D), B_W ** -0.5 * sub_scale)
    w_br_c = nrm((L, C_Q, D), C_Q ** -0.5 * sub_scale)
    w_out = nrm((L, D, D), D ** -0.5 * sub_scale)
    ln2_g = gain((L, D))
    ln2_b = nrm((L, D), 0.02)
    w_ff2_in = nrm((L, D, 2 * D_FF_2), D ** -0.5)
    w_ff2_out = nrm((L, D_FF_2, D), D_FF_2 ** -0.5 * sub_scale)
    ln3_g = gain((L, D))
    ln3_b = nrm((L, D), 0.02)
    return {'x': x, 'ln1_g': ln1_g, 'ln1_b': ln1_b, 'w_ff1_in': w_ff1_in, 'w_ff1_out': w_ff1_out,
            'w_in': w_in, 'b_in': b_in, 'conv_w': conv_w, 'a_log': a_log, 'dt_bias': dt_bias,
            'gdn_norm_g': gdn_norm_g, 'rel_bias': rel_bias, 'sinks': sinks, 'w_gate': w_gate,
            'b_gate': b_gate, 'w_br_a': w_br_a, 'w_br_b': w_br_b, 'w_br_c': w_br_c, 'w_out': w_out,
            'ln2_g': ln2_g, 'ln2_b': ln2_b, 'w_ff2_in': w_ff2_in, 'w_ff2_out': w_ff2_out,
            'ln3_g': ln3_g, 'ln3_b': ln3_b}

def second_block(x, ln1_g, ln1_b, w_ff1_in, w_ff1_out, w_in, b_in, conv_w, a_log, dt_bias,
              gdn_norm_g, rel_bias, sinks, w_gate, b_gate, w_br_a, w_br_b, w_br_c, w_out,
              ln2_g, ln2_b, w_ff2_in, w_ff2_out, ln3_g, ln3_b):
    alpha = (2.0 * DEPTH) ** 0.25
    for l in range(DEPTH):
        x = layer_norm(alpha * x + 0.5 * swiglu_2(x, w_ff1_in[l], w_ff1_out[l]), ln1_g[l], ln1_b[l])
        mix = hybrid_mixer(x, w_in[l], b_in[l], conv_w[l], a_log[l], dt_bias[l], gdn_norm_g[l],
                           rel_bias[l], sinks[l], w_gate[l], b_gate[l], w_br_a[l], w_br_b[l],
                           w_br_c[l], w_out[l])
        x = layer_norm(alpha * x + mix, ln2_g[l], ln2_b[l])
        x = layer_norm(alpha * x + 0.5 * swiglu_2(x, w_ff2_in[l], w_ff2_out[l]), ln3_g[l], ln3_b[l])
    return x


def setup_inputs(seed=0):
    out = dict(first_inputs(seed))
    for name, value in second_inputs(seed + 1).items():
        if name != "x":
            out[name + "_2"] = value
    return out


def reference(
    x, norm_mix, norm_ffn, even_w_in, gm_v_norm, gm_w_s, gm_b_s, mla_q_a_norm, mla_w_uq,
    mla_kv_a_norm, mla_w_ukv, mla_q_norm, mla_k_norm, even_w_out, odd_w_in, ret_out_norm,
    odd_w_out, ffn_w_gate, ffn_w_up, ffn_w_down, ln1_g_2, ln1_b_2, w_ff1_in_2, w_ff1_out_2,
    w_in_2, b_in_2, conv_w_2, a_log_2, dt_bias_2, gdn_norm_g_2, rel_bias_2, sinks_2, w_gate_2,
    b_gate_2, w_br_a_2, w_br_b_2, w_br_c_2, w_out_2, ln2_g_2, ln2_b_2, w_ff2_in_2, w_ff2_out_2,
    ln3_g_2, ln3_b_2,
):
    x = first_block(
        x, norm_mix, norm_ffn, even_w_in, gm_v_norm, gm_w_s, gm_b_s, mla_q_a_norm, mla_w_uq,
        mla_kv_a_norm, mla_w_ukv, mla_q_norm, mla_k_norm, even_w_out, odd_w_in, ret_out_norm,
        odd_w_out, ffn_w_gate, ffn_w_up, ffn_w_down,
    )
    return second_block(
        x, ln1_g_2, ln1_b_2, w_ff1_in_2, w_ff1_out_2, w_in_2, b_in_2, conv_w_2, a_log_2,
        dt_bias_2, gdn_norm_g_2, rel_bias_2, sinks_2, w_gate_2, b_gate_2, w_br_a_2, w_br_b_2,
        w_br_c_2, w_out_2, ln2_g_2, ln2_b_2, w_ff2_in_2, w_ff2_out_2, ln3_g_2, ln3_b_2,
    )


_drawn_inputs = setup_inputs


def setup_inputs(seed=0):
    import zlib

    import numpy as np

    out = dict(_drawn_inputs(seed))
    spreads = {}
    factors = {'mla_q_a_norm': 4.038,
     'mla_kv_a_norm': 2.821,
     'mla_k_norm': 3.88,
     'b_in_2': 8.0,
     'a_log_2': 4.578,
     'gdn_norm_g_2': 43.766,
     'rel_bias_2': 29.594,
     'sinks_2': 186.88,
     'b_gate_2': 8.0,
     'dt_bias_2': 2.832,
     'w_br_c_2': 2.714}
    for name, (base, spread) in spreads.items():
        noise = np.random.default_rng([zlib.crc32(name.encode()), seed]).standard_normal(out[name].shape)
        drawn = base * np.exp(spread * noise) if base else spread * noise
        out[name] = jnp.asarray(drawn.astype(out[name].dtype))
    for name, factor in factors.items():
        out[name] = (out[name] * factor).astype(out[name].dtype)
    return out
```

```python
from contextlib import ExitStack

import concourse.bass as bass
from concourse import mybir
import numpy as np

F32 = mybir.dt.float32
F32R = mybir.dt.float32r
U8 = mybir.dt.uint8
ALU = mybir.AluOpType
ACT = mybir.ActivationFunctionType
AX = mybir.AxisListType.X

NRAW, NHL, CW = 6, 5, 1024
ALPHA = float(4.0 ** 0.25)
NEG = -1e30
SQ2PI = float(np.sqrt(2.0 / np.pi))

PACK = [("nm0", 8), ("nm1", 8), ("nf0", 8), ("nf1", 8), ("gmv", 4), ("qan", 3), ("kvan", 2), ("ron", 16)]
for _l in range(2):
    PACK += [(f"l1g{_l}", 8), (f"l1b{_l}", 8), (f"l2g{_l}", 8), (f"l2b{_l}", 8), (f"l3g{_l}", 8), (f"l3b{_l}", 8),
             (f"bqa{_l}", 12), (f"bza{_l}", 4), (f"bqb{_l}", 4), (f"bkb{_l}", 4), (f"bqc{_l}", 4), (f"bkc{_l}", 1),
             (f"bg{_l}", 24), (f"cw{_l}", 48), (f"gng{_l}", 1)]
OFF, _n = {}, 0
for _name, _w in PACK:
    OFF[_name] = _n
    _n += _w
NPACK = _n
CONSTS = [("ident", 128), ("ones", 128), ("U", 128), ("nSU", 128), ("NEGU", 128), ("mask", 384), ("negd", 384),
          ("cc", 512), ("ss", 512), ("dtr", 1024), ("cosT", 32), ("sinT", 32)]
COFF, _n = {}, 0
for _name, _w in CONSTS:
    COFF[_name] = _n
    _n += _w
NCONST = _n
ROWC = 664


def act_(*a, **k):
    return lambda e: e.activation(*a, **k)


def tt_op(*a, **k):
    return lambda e: e.tensor_tensor(*a, **k)


def ts_op(*a, **k):
    return lambda e: e.tensor_scalar(*a, **k)


def stt_op(*a, **k):
    return lambda e: e.scalar_tensor_tensor(*a, **k)


def red_op(*a, **k):
    return lambda e: e.tensor_reduce(*a, **k)


def copy_op(*a, **k):
    return lambda e: e.tensor_copy(*a, **k)


def pred_op(*a, **k):
    return lambda e: e.copy_predicated(*a, **k)


def rcp_op(*a, **k):
    return lambda e: e.reciprocal(*a, **k)


def set_op(*a, **k):
    return lambda e: e.memset(*a, **k)


class Ch:

    def __init__(self, sem):
        self.sem, self.n = sem, 0


class Queue:

    def __init__(self, ch):
        self.items, self.seen, self.ch = [], {}, ch

    def wait(self, *tokens):
        for t in tokens:
            if t is None:
                continue
            if isinstance(t, list):
                self.wait(*t)
                continue
            ch, v = t
            if self.seen.get(id(ch), 0) < v:
                self.seen[id(ch)] = v
                self.items.append(lambda e, ch=ch, v=v: e.wait_ge(ch.sem, v))

    def do(self, fn, *tokens):
        self.wait(*tokens)
        ch = self.ch
        ch.n += 1
        self.items.append(lambda e: fn(e).then_inc(ch.sem, 1))
        return (ch, ch.n)

    def quiet(self, fn, *tokens):
        self.wait(*tokens)
        self.items.append(fn)

    def dma(self, ch, out, in_, *tokens):
        self.wait(*tokens)
        ch.n += 16
        self.items.append(lambda e: e.dma_start(out, in_).then_inc(ch.sem, 16))
        return (ch, ch.n)

    def last(self):
        return (self.ch, self.ch.n) if self.ch.n else None


class Bank:

    def __init__(self, t):
        self.t, self.rd = t, []

    def take(self):
        r, self.rd = self.rd, []
        return r


def emit(nc, ins, out, stop, order, dry):
    ctx = ExitStack()
    with ctx:
        def sb(name, shape, dt=F32):
            return ctx.enter_context(nc.sbuf_tensor(name, shape, dt))

        def chan(name):
            return Ch(ctx.enter_context(nc.semaphore(name)))

        raw = sb("raw", [128, NRAW, CW])
        whi = sb("whi", [128, NHL, CW], F32R)
        wlo = sb("wlo", [128, NHL, CW], F32R)
        x = sb("x", [128, 8, 256])
        xh = sb("xh", [128, 8, 256], F32R)
        xl = sb("xl", [128, 8, 256], F32R)
        h1 = [sb("h1h", [128, 4, 256], F32R), sb("h1l", [128, 4, 256], F32R)]
        h2 = [sb("h2h", [128, 4, 256], F32R), sb("h2l", [128, 4, 256], F32R)]
        t1 = sb("t1", [128, 4, 256])
        t2 = sb("t2", [128, 4, 256])
        R = sb("R", [128, 2, 256])
        pk = sb("pk", [128, NPACK])
        cst = sb("cst", [128, 640])
        lvm = sb("lvm", [128, 14, 128], U8)
        rowc = sb("rowc", [128, 704])
        epsc = sb("epsc", [128, 4])
        junk = sb("junk", [128, 1])[:, :]
        onm = sb("onm", [128, 128])[:, :]
        NAR = (nc.sbuf_bytes_remaining if not callable(nc.sbuf_bytes_remaining) else nc.sbuf_bytes_remaining()) // 4 - 64
        arena = sb("arena", [128, NAR])
        banks = [Bank(ctx.enter_context(nc.psum_tensor(f"ps{i}", [128, 512], F32))) for i in range(8)]

        ident, ones = cst[:, 0:128], cst[:, 128:256]
        Ucum, nSU, NEGU = cst[:, 256:384], cst[:, 384:512], cst[:, 512:640]

        pe, act, dve, pool, sp = (Queue(chan(f"s_{n}")) for n in ("pe", "act", "dve", "pool", "sp"))
        s_raw = [chan(f"s_raw{i}") for i in range(NRAW)]
        s_c = [chan(f"s_c{i}") for i in range(4)]
        s_tab = chan("s_tab")
        s_out = chan("s_out")

        apos = [0, 0]

        class Arena:

            def __init__(self):
                self.at = 0

            def get(self, *shape):
                n = int(np.prod(shape))
                v = arena[:, self.at:self.at + n]
                self.at += n
                apos[0] = max(apos[0], self.at)
                assert self.at <= NAR, (self.at, NAR)
                if len(shape) == 2:
                    v = v.rearrange("p (a b) -> p a b", b=shape[1])
                if len(shape) == 3:
                    v = v.rearrange("p (a b c) -> p a b c", b=shape[1], c=shape[2])
                return v

        def everyone():
            return [q.last() for q in (act, dve, pool)] + [apos_pe[0]]

        apos_pe = [None]

        def P(name, i=0, n=1):
            return pk[:, OFF[name] + i:OFF[name] + i + n]

        class Stream:
            def __init__(self):
                self.used, self.prepped, self.loaded, self.ndone = 0, 0, 0, 0
                self.hi_t, self.lo_t, self.raw_t, self.pe_t = {}, {}, {}, {}

            def load(self, upto):
                while self.loaded < min(upto, len(order)):
                    c = self.loaded
                    name, i = order[c]
                    src = ins[name]
                    w = src.shape[2]
                    prev = c - NRAW
                    self.raw_t[c] = sp.dma(s_raw[c % NRAW], raw[:, c % NRAW, 0:w], src[i],
                                           self.hi_t.get(prev), self.lo_t.get(prev))
                    self.loaded += 1

            def prep(self, upto):
                while self.prepped < min(upto, len(order)):
                    c = self.prepped
                    w = ins[order[c][0]].shape[2]
                    self.load(c + 1)
                    s, r = c % NHL, c % NRAW
                    self.hi_t[c] = act.do(act_(whi[:, s, 0:w], raw[:, r, 0:w], ACT.Copy),
                                          self.raw_t[c], self.pe_t.get(c - NHL))
                    self.lo_t[c] = dve.do(tt_op(
                        wlo[:, s, 0:w], raw[:, r, 0:w], whi[:, s, 0:w].bitcast(F32), ALU.subtract),
                        self.hi_t[c])
                    self.prepped += 1

            def next(self, name, i):
                c = self.used
                self.used += 1
                if dry:
                    order.append((name, i))
                    return whi[:, 0, :], wlo[:, 0, :]
                assert order[c] == (name, i)
                self.prep(self.ndone + NHL)
                self.load(self.ndone + NHL + NRAW)
                pe.wait(self.hi_t[c], self.lo_t[c])
                return whi[:, c % NHL, :], wlo[:, c % NHL, :]

            def done(self, tok, c=None):
                self.pe_t[self.used - 1 if c is None else c] = tok
                self.ndone += 1

        ws = Stream()
        side = []

        def step():
            for g in list(side):
                if next(g, "end") == "end":
                    side.remove(g)

        def finish():
            while side:
                step()

        def mm(out, lhsT, rhs, start=True, stop=True, mark=False, waits=()):
            def fn(e):
                return e.matmul(out, lhsT, rhs, start=start, stop=stop, skip_group_check=True)
            if mark:
                apos_pe[0] = pe.do(fn, *waits)
                return apos_pe[0]
            pe.quiet(fn, *waits)

        def tr(out, in_, idn, mark=False, waits=()):
            def fn(e):
                return e.transpose(out, in_, idn)
            if mark:
                apos_pe[0] = pe.do(fn, *waits)
                return apos_pe[0]
            pe.quiet(fn, *waits)

        def mm3(out, wh, wl, ah, al, start, stop, first, mark):
            mm(out, wh, ah, start=start, stop=False)
            mm(out, wl, ah, start=False, stop=False)
            return mm(out, wh, al, start=False, stop=stop, mark=mark)

        def gemm_fm(name, i, bank, half, ah, al, K=8, woff=0, fetch=True, wv=None, waits=(), first=None):
            if wv is None:
                wv = ws.next(name, i)
            wh, wl = wv
            o = bank.t[:, half * 256:half * 256 + 256]
            pe.wait(bank.take(), *waits)
            for k in range(K):
                c = woff + k * 128
                t = mm3(o, wh[:, c:c + 128], wl[:, c:c + 128], ah[:, k, :], al[:, k, :],
                        k == 0, k == K - 1, None, k == K - 1)
            ws.done(t)
            return t

        def gemm_fm_first(specs, ah, al, wk):
            c0 = ws.used
            wv = [ws.next(n, i) for n, i, _, _ in specs]
            toks = []
            for n, i, bank, half in specs:
                pe.wait(bank.take())
            for k in range(8):
                pe.wait(*wk[k])
                for m, (n, i, bank, half) in enumerate(specs):
                    c = k * 128
                    t = mm3(bank.t[:, half * 256:half * 256 + 256], wv[m][0][:, c:c + 128], wv[m][1][:, c:c + 128],
                            ah[:, k, :], al[:, k, :], k == 0 and half == 0, k == 7, None, k == 7)
                    if k == 7:
                        toks.append(t)
                        ws.done(t, c0 + m)
            return toks

        def gemm_tm(name, i0, bks, ah, al, K, kper, n, woff=0, waits=(), col=0, after=None, wk=None):
            for b in bks:
                pe.wait(b.take())
            pe.wait(*waits)
            for c in range(K // kper):
                wh, wl = ws.next(name, i0 + c)
                for kk in range(kper):
                    k = c * kper + kk
                    if wk is not None:
                        pe.wait(*wk[k])
                    w0 = woff + kk * n
                    for tt in range(2):
                        b = bks[tt % len(bks)]
                        co = col + (n * tt if len(bks) == 1 else 0)
                        o = b.t[:, co:co + n]
                        s = slice(tt * 128, tt * 128 + 128)
                        st = k == 0
                        mm(o, ah[:, k, s], wh[:, w0:w0 + n], start=st and (len(bks) == 2 or tt == 0), stop=False)
                        mm(o, al[:, k, s], wh[:, w0:w0 + n], start=False, stop=False)
                        t = mm(o, ah[:, k, s], wl[:, w0:w0 + n], start=False, stop=k == K - 1,
                               mark=kk == kper - 1 and tt == 1)
                ws.done(t)
                if after:
                    after()
            return t

        def gemm_acc(name, i, ah, al, k, first, last, waits=(), kk=None):
            wh, wl = ws.next(name, i)
            pe.wait(*waits)
            toks = []
            for n in range(8):
                b = banks[n // 2]
                if first and n % 2 == 0:
                    pe.wait(b.take())
                o = b.t[:, (n % 2) * 256:(n % 2) * 256 + 256]
                t = mm3(o, wh[:, n * 128:n * 128 + 128], wl[:, n * 128:n * 128 + 128], ah[:, k, :], al[:, k, :],
                        first and n % 2 == 0, last, None, n == 7 or (last and n % 2 == 1))
                if n % 2 == 1:
                    toks.append(t)
            ws.done(t)
            return toks

        def split(src, dh, dl, g=None, waits=(), n=1):
            if g is None:
                a = act.do(act_(dh, src, ACT.Copy), *waits)
                d = dve.do(tt_op(dl, src, dh.bitcast(F32), ALU.subtract), a, *waits)
            else:
                a = act.do(act_(dh, src, ACT.Copy, scale=g), *waits)
                d = dve.do(stt_op(dl, src, g, dh.bitcast(F32), ALU.mult, ALU.subtract), a, *waits)
            return [a, d]

        def rstd_of(ps, dst, eps, tmp, tok, bank=None, scale=1.0):
            a = act.do(act_(tmp, ps, ACT.Sqrt, bias=eps, scale=scale), tok)
            if bank is not None:
                bank.rd.append(a)
            return dve.do(rcp_op(dst, tmp), a)

        def presum(src4, toks, acc):
            t = dve.do(tt_op(acc, src4[0], src4[1], ALU.add), toks[0], toks[1])
            t = dve.do(tt_op(acc, acc, src4[2], ALU.add), t, toks[2])
            return dve.do(tt_op(acc, acc, src4[3], ALU.add), t, toks[3])

        sqs = [t1[:, 0:2, :], t1[:, 2:4, :], t2[:, 0:2, :], t2[:, 2:4, :]]

        def add_pair(p, tok, alpha):
            b = banks[p]
            v = x[:, 2 * p:2 * p + 2, :]
            src = b.t[:, :].rearrange("p (a b) -> p a b", b=256)
            t = dve.do(stt_op(v, v, alpha, src, ALU.mult, ALU.add), tok)
            b.rd.append(t)
            return t

        def prefetch(fn):
            act.do(act_(junk, epsc[:, 0:1], fn), *me)

        def rms_parts(gname, toks, xt=None):
            fr = everyone() if xt is not None else []
            pt, sp_t = [], []
            for p in range(4):
                a = add_pair(p, toks[p], 1.0) if xt is None else xt[p]
                pt.append(a)
                for k in (2 * p, 2 * p + 1):
                    sp_t.append(split(x[:, k, :], xh[:, k, :], xl[:, k, :], P(gname, k) if gname else None, waits=[a, fr]))
            if gname is None:
                return sp_t, None, None
            prefetch(ACT.Sqrt)
            for p in range(4):
                pt[p] = act.do(act_(sqs[p], x[:, 2 * p:2 * p + 2, :], ACT.Square), pt[p], fr)
            return sp_t, presum(sqs, pt, sqs[0]), pt

        def rms_stats(t, RT=None, nxt=None):
            acc = sqs[0]
            b = banks[7]
            pe.wait(b.take(), t)
            mm(b.t[:, 0:256], onm, acc[:, 0, :], start=True, stop=False)
            t = mm(b.t[:, 0:256], onm, acc[:, 1, :], start=False, stop=True, mark=True)
            a = act.do(act_(sqs[1][:, 0, :], b.t[:, 0:256], ACT.Sqrt, bias=epsc[:, 0:1]), t)
            r = [dve.do(rcp_op(R[:, 0, :], sqs[1][:, 0, :]), a)]
            b.rd.append(a)
            if RT is not None:
                b7 = banks[6]
                pe.wait(b7.take())
                for tt in range(2):
                    s = slice(tt * 128, tt * 128 + 128)
                    mm(b7.t[:, tt:tt + 1], acc[:, 0, s], onm[:, 0:1], start=True, stop=False)
                    t = mm(b7.t[:, tt:tt + 1], acc[:, 1, s], onm[:, 0:1], start=False, stop=True, mark=True)
                a = act.do(act_(epsc[:, 2:4], b7.t[:, 0:2], ACT.Sqrt, bias=epsc[:, 0:1]), t)
                b7.rd.append(a)
                r.append(dve.do(rcp_op(RT, epsc[:, 2:4]), a))
            if nxt is not None:
                prefetch(nxt)
            return r

        def layer_norm(gname, bname, toks, final=False, nxt=ACT.Silu):
            acc = t1[:, 0:2, :]
            yt = [add_pair(0, toks[0], ALPHA), add_pair(1, toks[1], ALPHA)]
            t = dve.do(tt_op(acc, x[:, 0:2, :], x[:, 2:4, :], ALU.add), yt[0], yt[1], *everyone())
            yt.append(add_pair(2, toks[2], ALPHA))
            t = dve.do(tt_op(acc, acc, x[:, 4:6, :], ALU.add), t, yt[2])
            yt.append(add_pair(3, toks[3], ALPHA))
            prefetch(ACT.Sqrt)
            b = banks[6]
            pe.wait(b.take(), t)
            mm(b.t[:, 0:256], onm, acc[:, 0, :], start=True, stop=False)
            mm(b.t[:, 0:256], onm, acc[:, 1, :], start=False, stop=False)
            pe.wait(yt[3])
            mm(b.t[:, 0:256], onm, x[:, 6, :], start=False, stop=False)
            m = mm(b.t[:, 0:256], onm, x[:, 7, :], start=False, stop=True, mark=True)
            mean = b.t[:, 0:256].unsqueeze(1).broadcast_to([128, 2, 256])
            b7 = banks[7]
            pe.wait(b7.take())
            qt = []
            for p in range(4):
                v = x[:, 2 * p:2 * p + 2, :]
                ct = dve.do(tt_op(v, v, mean, ALU.subtract), m, yt[p])
                qt.append(act.do(act_(sqs[p], v, ACT.Square), ct, m))
                for i in range(2):
                    t = mm(b7.t[:, 0:256], onm, sqs[p][:, i, :], start=p == 0 and i == 0, stop=p == 3 and i == 1,
                           mark=p == 3 and i == 1, waits=[qt[-1]])
            b.rd.append(ct)
            a = act.do(act_(R[:, 0, :], b7.t[:, 0:256], ACT.Sqrt, bias=epsc[:, 1:2]), t)
            b7.rd.append(a)
            r = dve.do(rcp_op(R[:, 1, :], R[:, 0, :]), a)
            prefetch(nxt)
            out_t, hi = [], []
            for k in range(9):
                if k < 8:
                    nt = dve.do(stt_op(x[:, k, :], x[:, k, :], P(gname, k), R[:, 1, :], ALU.mult, ALU.mult), r, qt[k // 2])
                    if final:
                        out_t.append([dve.do(ts_op(x[:, k, :], x[:, k, :], P(bname, k), None, ALU.add), nt)])
                        continue
                    hi.append(act.do(act_(xh[:, k, :], x[:, k, :], ACT.Identity, bias=P(bname, k)), nt))
                if k > 0 and not final:
                    j = k - 1
                    lo = dve.do(stt_op(xl[:, j, :], x[:, j, :], P(bname, j), xh[:, j, :].bitcast(F32), ALU.add, ALU.subtract), hi[j])
                    out_t.append([hi[j], lo])
            if not final:
                for k in range(8):
                    pool.do(ts_op(x[:, k, :], x[:, k, :], P(bname, k), None, ALU.add), out_t[k])
            xready[0] = pool.last()
            return out_t

        xready = [None]

        def ffn(wg, wu, wd, NT, xt, stats=None, half=1.0):
            Rt = None
            ht = {}
            dt_ = {}
            toks = None
            used = {}
            for j in range(NT + 2):
                if j < NT:
                    b = banks[4 + j % 4]
                    if j == 0:
                        early = gemm_fm_first([(wg, 0, b, 0), (wu, 0, b, 1), (wg, 1, banks[5], 0), (wu, 1, banks[5], 1)],
                                              xh, xl, xt)
                        tu = early[3]
                        if stats is not None:
                            Rt = stats()
                    elif j == 1:
                        tu = early[3]
                    else:
                        gemm_fm(wg, j, b, 0, xh, xl)
                        tu = gemm_fm(wu, j, b, 1, xh, xl)
                    q = j % 4
                    s, u = t1[:, q, :], t2[:, q, :]
                    hh, hl = h1[0][:, q, :], h1[1][:, q, :]
                    G, U_ = b.t[:, 0:256], b.t[:, 256:512]
                    prev = ht.get(j - 4)
                    if Rt is not None:
                        a = dve.do(tt_op(s, G, R[:, 0, :], ALU.mult), tu, Rt, prev)
                        a = act.do(act_(s, s, ACT.Silu), a)
                        a = dve.do(tt_op(s, s, R[:, 0, :], ALU.mult), a)
                        a = dve.do(tt_op(u, s, U_, ALU.mult), a)
                    else:
                        a = act.do(act_(s, G, ACT.Silu), tu, prev)
                        a = dve.do(stt_op(u, s, half, U_, ALU.mult, ALU.mult), a)
                    b.rd.append(a)
                    ht[j] = split(u, hh, hl, waits=[a, dt_.get(j - 4)])
                if j >= 2:
                    k = j - 2
                    toks = gemm_acc(wd, k, h1[0], h1[1], k % 4, k == 0, k == NT - 1, waits=ht[k])
                    dt_[k] = toks[-1]
            return toks

        def attend(nh, qf, kf, vf, bias, S, PT, st, bks, put, scale, sink=None, fr=(), slope=None, ready=(), gap=2):
            for h0 in range(0, nh, 4):
                stt = []
                for i in range(4):
                    h = h0 + i
                    b = bks[i % 2]
                    pe.wait(b.take(), *ready)
                    q, k = qf(h), kf(h)
                    mm(b.t[:, 0:128], q[:, 0:128], k[:, 0:128])
                    t = mm(b.t[:, 128:384], q[:, 128:256], k[:, 0:256], mark=True)
                    if slope is None:
                        bi = bias(h)
                        a = dve.do(stt_op(
                            S[:, i, :], b.t[:, 0:384], scale, bi, ALU.mult, ALU.add), t, *fr)
                    else:
                        a = dve.do(stt_op(
                            S[:, i, :], bias(h), slope(h), b.t[:, 0:384], ALU.mult, ALU.add), t, *fr)
                    b.rd.append(a)
                    stt.append(a)
                    if i % 2 == 1:
                        yield
                m = dve.do(red_op(st[:, 0, 0:4], S[:, :, 0:128], AX, ALU.max), *stt)
                m2 = dve.do(red_op(st[:, 0, 4:8], S[:, :, 128:384], AX, ALU.max), *stt)
                if sink is not None:
                    sk = sink(h0)
                    m = dve.do(tt_op(
                        st[:, 0, :].rearrange("p (a b) -> p a b", b=4), st[:, 0, :].rearrange("p (a b) -> p a b", b=4),
                        sk.unsqueeze(1).broadcast_to([128, 2, 4]), ALU.max), m, m2)
                m = dve.do(ts_op(st[:, 1, :], st[:, 0, :], -1.0, None, ALU.mult), m, m2)
                ex = []
                for i in range(4):
                    for sgm, sl in ((0, slice(0, 128)), (1, slice(128, 384))):
                        c = sgm * 4 + i
                        ex.append(act.do(act_(
                            S[:, i, sl], S[:, i, sl], ACT.Exp, bias=st[:, 1, c:c + 1], accum_out=st[:, 2, c:c + 1]), m))
                if sink is not None:
                    z = dve.do(tt_op(
                        st[:, 4, :].rearrange("p (a b) -> p a b", b=4), sk.unsqueeze(1).broadcast_to([128, 2, 4]),
                        st[:, 1, :].rearrange("p (a b) -> p a b", b=4), ALU.add), m)
                    z = act.do(act_(st[:, 4, :], st[:, 4, :], ACT.Exp), z)
                    z = dve.do(tt_op(st[:, 2, :], st[:, 2, :], st[:, 4, :], ALU.add), z, *ex)
                else:
                    z = ex[-1]
                for _ in range(gap):
                    yield
                r = dve.do(rcp_op(st[:, 3, :], st[:, 2, :]), z)
                n1 = dve.do(tt_op(S[:, :, 0:128], S[:, :, 0:128],
                                                      st[:, 3, 0:4].unsqueeze(2).broadcast_to([128, 4, 128]), ALU.mult), r, *ex)
                n2 = dve.do(tt_op(S[:, :, 128:384], S[:, :, 128:384],
                                                      st[:, 3, 4:8].unsqueeze(2).broadcast_to([128, 4, 256]), ALU.mult), r, *ex)
                yield
                yield
                pts = []
                for i in range(4):
                    b = bks[i % 2]
                    pe.wait(b.take(), n1, n2)
                    for j in range(3):
                        t = tr(b.t[:, j * 128:j * 128 + 128], S[:, i, j * 128:j * 128 + 128], ident, mark=j == 2)
                    a = act.do(act_(PT[:, i, :], b.t[:, 0:384], ACT.Copy), t)
                    b.rd.append(a)
                    pts.append(a)
                    if i % 2 == 1:
                        yield
                for i in range(4):
                    put(h0 + i, PT[:, i, :], vf(h0 + i), pts[i])
                    if i % 2 == 1:
                        yield

        def pv(o, pt, v, wait):
            mm(o, v[0], pt[:, 0:256], start=True, stop=False, waits=wait)
            return mm(o[:, 128:256], v[1], pt[:, 256:384], start=False, stop=True, mark=True)

        c = ins["consts"]
        tc = sp.dma(s_c[0], cst[:, :], c[:, 0:640])
        tp = sp.dma(s_c[1], pk[:, :], ins["pack"])
        lvf = arena[:, 2048:2048 + 1792].rearrange("p (a b) -> p a b", b=128)
        tl = sp.dma(s_c[2], lvf, ins["lvmask"])
        tl = dve.do(copy_op(lvm[:, :, :], lvf), tl)
        ar = Arena()
        xtm = ar.get(2, 1024)
        tx = sp.dma(s_c[3], xtm, ins["x"].rearrange("(a p) d -> p a d", p=128))
        me = [dve.do(set_op(epsc[:, 0:1], 1e-6)), dve.do(set_op(epsc[:, 1:2], 1e-5)), dve.do(set_op(onm, 1.0 / 1024))]
        for q in (act, pe):
            q.wait(*me)
        for q in (act, dve, sp):
            q.wait(tp, tl)
        xt = []
        for p in range(4):
            b = banks[p]
            pe.wait(tc, tx)
            for kk in range(2):
                for tt in range(2):
                    t = tr(b.t[:, kk * 256 + tt * 128:kk * 256 + tt * 128 + 128],
                           xtm[:, tt, (2 * p + kk) * 128:(2 * p + kk + 1) * 128], ident, mark=kk == 1 and tt == 1)
            a = dve.do(copy_op(
                x[:, 2 * p:2 * p + 2, :], b.t[:, :].rearrange("p (a b) -> p a b", b=256)), t)
            b.rd.append(a)
            xt.append(a)

        def even(xt):
            RT = ar.get(2)
            cq, ckv = ar.get(3, 256), ar.get(2, 256)
            kpe = ar.get(2, 32)
            qkT = ar.get(32, 96)
            kvT = ar.get(2, 1024)
            uF, vT = ar.get(4, 256), ar.get(2, 512)
            gw, gwT = ar.get(4, 128), ar.get(4, 128)
            qF, kF = ar.get(8, 256), ar.get(8, 256)
            S, PT, st = ar.get(4, 384), ar.get(4, 384), ar.get(5, 8)
            sq = ar.get(5, 256)
            rr = ar.get(64)
            cs = ar.get(2, 32)
            mk = ar.get(384)
            twk = ar.get(4, 256)
            sqt = arena[:, 0:2048]
            oF = arena[:, 0:1024].rearrange("p (a b) -> p a b", b=256)
            s_e = chan("s_e")
            t_row = sp.dma(s_e, rowc[:, 0:704], ins["rowa"].partition_broadcast(128))
            t_gw = sp.dma(chan("s_e2"), gw, ins["gmw"].rearrange("g t s -> t g s"))
            t_cs = sp.dma(chan("s_e3"), cs, c[:, COFF["cosT"]:COFF["cosT"] + 64].rearrange("p (a b) -> p a b", b=32))
            t_mk = sp.dma(chan("s_e4"), mk, c[:, COFF["mask"]:COFF["mask"] + 384])
            sp_t, sqt_, _ = rms_parts("nm0", None, xt)
            rt = rms_stats(sqt_, RT)
            ah, al = xh, xl
            wt = []
            for s_ in sp_t:
                wt += s_
            toks = []
            for i in range(5):
                b = banks[i % 4]
                t = gemm_fm("ew_c", i, b, 0, ah, al, waits=wt)
                dst = cq[:, i, :] if i < 3 else ckv[:, i - 3, :]
                a = dve.do(tt_op(dst, b.t[:, 0:256], R[:, 0, :], ALU.mult), t, *rt)
                b.rd.append(a)
                q = act.do(act_(sq[:, i, :], dst, ACT.Square), a)
                toks.append([a, q])
            b = banks[4]
            t = gemm_tm("ew_pe", 0, [b], ah, al, 8, 8, 32)
            a = dve.do(tt_op(kpe, b.t[:, 0:64].rearrange("p (a b) -> p a b", b=32),
                                                 RT.unsqueeze(2).broadcast_to([128, 2, 32]), ALU.mult), t)
            b.rd.append(a)
            t_kpe = a
            sqd = []
            for i in range(5):
                dst = cq[:, i, :] if i < 3 else ckv[:, i - 3, :]
                g = P("qan", i) if i < 3 else P("kvan", i - 3)
                hh = h1[0][:, i, :] if i < 3 else h2[0][:, i - 3, :]
                hl = h1[1][:, i, :] if i < 3 else h2[1][:, i - 3, :]
                sqd.append(split(dst, hh, hl, g, waits=toks[i]))
            b = banks[5]
            pe.wait(b.take(), *[tt[1] for tt in toks])
            for kind, ks in ((0, (0, 1, 2)), (1, (3, 4))):
                for tt in range(2):
                    s = slice(tt * 128, tt * 128 + 128)
                    col = kind * 2 + tt
                    for k in ks:
                        t = mm(b.t[:, col:col + 1], sq[:, k, s], ones[:, 0:1], start=k == ks[0], stop=k == ks[-1], mark=True)
            a1 = act.do(act_(rr[:, 0:2], b.t[:, 0:2], ACT.Sqrt, bias=epsc[:, 0:1], scale=1.0 / 384), t)
            a2 = act.do(act_(rr[:, 2:4], b.t[:, 2:4], ACT.Sqrt, bias=epsc[:, 0:1], scale=1.0 / 256), t)
            b.rd += [a1, a2]
            t_rr = dve.do(rcp_op(rr[:, 4:8], rr[:, 0:4]), a1, a2)
            for i in range(4):
                b = banks[i % 4]
                t = gemm_fm("ew_u", i, b, 0, ah, al)
                a = dve.do(tt_op(uF[:, i, :], b.t[:, 0:256], R[:, 0, :], ALU.mult), t)
                b.rd.append(a)
                ug = act.do(act_(uF[:, i, :], uF[:, i, :], ACT.Gelu_apprx_tanh), a)
            t = gemm_tm("ew_v", 0, [banks[6], banks[7]], ah, al, 8, 2, 512)
            vt = []
            for tt in range(2):
                b = banks[6 + tt]
                vt.append(act.do(act_(vT[:, tt, :], b.t[:, :], ACT.Gelu_apprx_tanh,
                                                                  scale=RT[:, tt:tt + 1]), t, *rt))
                b.rd.append(vt[-1])
            kk_t = []
            for half in range(2):
                t = gemm_tm("ew_ukv", half, [banks[0], banks[1]], h2[0], h2[1], 2, 2, 512, waits=sqd[3] + sqd[4])
                for tt in range(2):
                    b = banks[tt]
                    a = act.do(act_(
                        kvT[:, tt, half * 512:half * 512 + 512], b.t[:, :], ACT.Copy, scale=rr[:, 6 + tt:7 + tt]), t, t_rr)
                    b.rd.append(a)
                    kk_t.append(a)
            for cg in range(3):
                bq = [banks[2], banks[3]] if cg % 2 == 0 else [banks[4], banks[5]]
                t = gemm_tm("ew_uq", cg, bq, h1[0], h1[1], 3, 3, 256, waits=sqd[0] + sqd[1] + sqd[2])
                for tt in range(2):
                    b = bq[tt]
                    dst = qkT[:, tt * 8:tt * 8 + 8, :].rearrange("p a b -> p (a b)")[:, cg * 256:cg * 256 + 256]
                    a = act.do(act_(
                        dst, b.t[:, 0:256], ACT.Copy, scale=rr[:, 4 + tt:5 + tt]), t, t_rr)
                    b.rd.append(a)
                    kk_t.append(a)
            dve.wait(t_row)
            dve.wait(t_cs)
            for tt in range(2):
                kk_t.append(dve.do(copy_op(
                    qkT[:, 16 + tt * 8:24 + tt * 8, 0:64], kvT[:, tt, :].rearrange("p (h d) -> p h d", d=128)[:, :, 0:64]), *kk_t))
                kk_t.append(dve.do(copy_op(
                    qkT[:, 16 + tt * 8:24 + tt * 8, 64:96], kpe[:, tt, :].unsqueeze(1).broadcast_to([128, 8, 32])), t_kpe))
            hn = []
            for hf in range(2):
                v = qkT[:, hf * 16:hf * 16 + 16, :]
                sv = sqt[:, 0:1536].rearrange("p (a b) -> p a b", b=96)
                a = act.do(act_(sv, v, ACT.Square), *kk_t, *hn[-1:])
                a = dve.do(red_op(rr[:, 8 + hf * 16:24 + hf * 16], sv, AX, ALU.add), a)
                hn.append(a)
            a = act.do(act_(sqt[:, 0:32], rr[:, 8:40], ACT.Sqrt, bias=epsc[:, 0:1], scale=1.0 / 96), *hn)
            a = dve.do(rcp_op(rr[:, 8:40], sqt[:, 0:32]), a)
            a = dve.do(tt_op(qkT, qkT, rr[:, 8:40].unsqueeze(2).broadcast_to([128, 32, 96]), ALU.mult), a, *kk_t)
            qk_t = []
            for w in range(2):
                v = qkT[:, w * 16:w * 16 + 16, :]
                g = rowc[:, w * 96:w * 96 + 96].unsqueeze(1).broadcast_to([128, 16, 96])
                a2 = dve.do(tt_op(v, v, g, ALU.mult), a)
                x1 = qkT[:, w * 16:w * 16 + 16, 64:80].rearrange("p (t h) d -> p t h d", t=2)
                x2 = qkT[:, w * 16:w * 16 + 16, 80:96].rearrange("p (t h) d -> p t h d", t=2)
                C = cs[:, 0, :].rearrange("p (t d) -> p t d", t=2).unsqueeze(2).broadcast_to([128, 2, 8, 16])
                Sn = cs[:, 1, :].rearrange("p (t d) -> p t d", t=2).unsqueeze(2).broadcast_to([128, 2, 8, 16])
                tm = [twk[:, i, 0:256].rearrange("p (t h d) -> p t h d", t=2, h=8) for i in range(4)]
                m1 = dve.do(tt_op(tm[0], x1, C, ALU.mult), a2, *qk_t)
                m2 = dve.do(tt_op(tm[1], x2, Sn, ALU.mult), a2)
                m3 = dve.do(tt_op(tm[2], x2, C, ALU.mult), a2)
                m4 = dve.do(tt_op(tm[3], x1, Sn, ALU.mult), a2)
                dve.do(tt_op(x1, tm[0], tm[1], ALU.subtract), m1, m2, m3, m4)
                qk_t = [dve.do(tt_op(x2, tm[2], tm[3], ALU.add), m3, m4)]
            v8 = vT.rearrange("p t (g d) -> p (t g) d", d=128)
            s8 = sqt[:, 0:1024].rearrange("p (a b) -> p a b", b=128)
            a = act.do(act_(s8, v8, ACT.Square), *vt, a)
            a = dve.do(red_op(rr[:, 40:48], s8, AX, ALU.add), a)
            a = act.do(act_(rr[:, 48:56], rr[:, 40:48], ACT.Sqrt, bias=epsc[:, 0:1], scale=1.0 / 128), a)
            a = dve.do(rcp_op(rr[:, 40:48], rr[:, 48:56]), a)
            t_v = dve.do(tt_op(v8, v8, rr[:, 40:48].unsqueeze(2).broadcast_to([128, 8, 128]), ALU.mult), a)
            b = banks[6]
            pe.wait(b.take(), t_gw)
            for g in range(4):
                t = tr(b.t[:, g * 128:g * 128 + 128], gw[:, g, :], ident, mark=g == 3)
            a = act.do(act_(gwT, b.t[:, :].rearrange("p (a b) -> p a b", b=128), ACT.Copy), t)
            b.rd.append(a)
            t_gw = dve.do(set_op(gwT[64:128, :, 0:64], 0.0), a)
            at_t = []
            for g in range(4):
                b = banks[g]
                pe.wait(b.take(), t_v, t_gw)
                for n in range(2):
                    t = mm(b.t[:, n * 128:n * 128 + 128], vT[:, n, g * 128:g * 128 + 128], gwT[:, g, :],
                           mark=n == 1)
                tw = twk[:, g, 0:256]
                bB = rowc[:, 192 + g * 128:192 + g * 128 + 128].unsqueeze(1).broadcast_to([128, 2, 128])
                a = dve.do(stt_op(
                    tw.rearrange("p (a b) -> p a b", b=128), b.t[:, 0:256].rearrange("p (a b) -> p a b", b=128),
                    P("gmv", g), bB, ALU.mult, ALU.add), t, *qk_t)
                b.rd.append(a)
                a = dve.do(tt_op(tw, tw, uF[:, g, :], ALU.mult), a, ug)
                at_t.append(split(tw, h1[0][:, g, :], h1[1][:, g, :], waits=[a, apos_pe[0]]))
            tf = []
            for w, dst in ((0, qF), (1, kF)):
                for h2_ in range(0, 8, 2):
                    b = banks[4 + (h2_ // 2) % 4]
                    pe.wait(b.take(), *qk_t)
                    for hh in range(2):
                        for tt in range(2):
                            t = tr(b.t[0:96, hh * 256 + tt * 128:hh * 256 + tt * 128 + 128],
                                   qkT[:, w * 16 + tt * 8 + h2_ + hh, :], ident, mark=hh == 1 and tt == 1)
                    a = act.do(act_(
                        dst[0:96, h2_:h2_ + 2, :], b.t[0:96, :].rearrange("p (a b) -> p a b", b=256), ACT.Copy), t)
                    b.rd.append(a)
                    tf.append(a)
            ot = {}

            def put(h, pt, v, w):
                j = h // 2
                b = banks[6 + j % 2]
                if h % 2 == 0:
                    pe.wait(b.take())
                p0 = 64 * (h % 2)
                t = pv(b.t[p0:p0 + 64, 0:256], pt, v, [w])
                if h % 2 == 1:
                    a = act.do(act_(oF[:, j, :], b.t[:, 0:256], ACT.Copy), t)
                    b.rd.append(a)
                    ot[j] = split(oF[:, j, :], h2[0][:, j, :], h2[1][:, j, :], waits=[a])

            dve.wait(t_mk)
            side.append(attend(8, lambda h: qF[0:96, h, :], lambda h: kF[0:96, h, :],
                               lambda h: [kvT[:, n, h * 128 + 64:h * 128 + 128] for n in range(2)],
                               lambda h: mk, S, PT, st, [banks[4], banks[5]], put, float(96 ** -0.5), ready=tf))
            step()
            for k in range(4):
                gemm_acc("ew_out", k, h1[0], h1[1], k, k == 0, False, waits=at_t[k])
                step()
            finish()
            for k in range(4):
                toks = gemm_acc("ew_out", 4 + k, h2[0], h2[1], k, False, k == 3, waits=ot[k])
            return toks

        def odd(xt):
            ar = Arena()
            fr = everyone()
            RT = ar.get(2)
            qF, kF = ar.get(8, 256), ar.get(8, 256)
            vT = ar.get(2, 2048)
            sg = ar.get(16, 256)
            cc, ss = ar.get(2, 256), ar.get(2, 256)
            dtr = ar.get(4, 256)
            AT = ar.get(2, 384)
            o = ar.get(4, 256)
            osq = ar.get(4, 256)
            tq = ar.get(2, 512)
            Ro = ar.get(2, 256)
            s_o = [chan(f"s_o{i}") for i in range(3)]
            tb = [sp.dma(s_o[0], cc, c[:, COFF["cc"]:COFF["cc"] + 512].rearrange("p (a b) -> p a b", b=256), fr),
                  sp.dma(s_o[1], ss, c[:, COFF["ss"]:COFF["ss"] + 512].rearrange("p (a b) -> p a b", b=256), fr),
                  sp.dma(s_o[2], dtr, c[:, COFF["dtr"]:COFF["dtr"] + 1024].rearrange("p (a b) -> p a b", b=256), fr)]
            dve.wait(*fr)
            act.wait(*fr)
            sp_t, sqt_, _ = rms_parts("nm1", xt)
            rt = ()
            vt = []
            for cg in range(4):
                bq = [banks[0], banks[1]] if cg % 2 == 0 else [banks[2], banks[3]]
                t = gemm_tm("ow_v", cg * 4, bq, xh, xl, 8, 2, 512, wk=sp_t)
                if cg == 0:
                    rt = rms_stats(sqt_, RT)
                for tt in range(2):
                    b = bq[tt]
                    a = act.do(act_(
                        vT[:, tt, cg * 512:cg * 512 + 512], b.t[:, :], ACT.Copy, scale=RT[:, tt:tt + 1]), t, *rt)
                    b.rd.append(a)
                    vt.append(a)
            dve.wait(*tb)
            qt = {}
            prev = None
            for i in range(8):
                h, w = i // 2, i % 2
                b = banks[4 + i % 2]
                gemm_fm("ow_qk", 2 * i, b, 0, xh, xl)
                t = gemm_fm("ow_qk", 2 * i + 1, b, 1, xh, xl)
                tt_ = tq[:, 0, :].rearrange("p (a b) -> p a b", b=256)
                ts_ = tq[:, 1, :].rearrange("p (a b) -> p a b", b=256)
                a = dve.do(tt_op(
                    tt_, b.t[:, :].rearrange("p (a b) -> p a b", b=256), R[:, 0:1, :].broadcast_to([128, 2, 256]), ALU.mult), t, prev, *rt)
                b.rd.append(a)
                s0 = dve.do(tt_op(ts_[:, 0, :], tt_[:, 1, :], ss[:, 0, :], ALU.mult), a)
                s1 = dve.do(tt_op(ts_[:, 1, :], tt_[:, 0, :], ss[:, 1, :], ALU.mult), a)
                a = dve.do(tt_op(tt_, tt_, cc, ALU.mult), s0, s1)
                dst = (qF if w == 0 else kF)[:, 2 * h:2 * h + 2, :]
                prev = dve.do(tt_op(dst, tt_, ts_, ALU.add), a)
                qt[h, w] = prev
            gt = {}
            ot = {}
            hb = [h1, h2]
            ows = {}

            def head(h):
                b = banks[5]
                pe.wait(b.take(), qt[h, 0], qt[h, 1])
                for d in range(2):
                    mm(b.t[:, 0:256], kF[:, 2 * h + d, 0:128], qF[:, 2 * h + d, :], start=d == 0, stop=d == 1)
                for d in range(2):
                    t = mm(b.t[:, 256:384], kF[:, 2 * h + d, 128:256], qF[:, 2 * h + d, 128:256], start=d == 0, stop=d == 1, mark=True)
                a = dve.do(stt_op(
                    AT[:, h % 2, 0:256], b.t[:, 0:256], 0.0625, dtr[:, h, :], ALU.mult, ALU.mult), t, ot.get((h - 2, "pe")))
                a2 = dve.do(stt_op(
                    AT[:, h % 2, 256:384], b.t[:, 256:384], 0.0625, dtr[:, h, 0:128], ALU.mult, ALU.mult), t)
                b.rd.append(a2)
                yield
                ev = []
                for pr in range(2):
                    b = banks[6 + pr]
                    pe.wait(b.take(), a, a2, *vt)
                    for e_ in range(2):
                        ec = h * 512 + (pr * 2 + e_) * 128
                        ob = b.t[:, e_ * 256:e_ * 256 + 256]
                        mm(ob, vT[:, 0, ec:ec + 128], AT[:, h % 2, 0:256], start=e_ == 0, stop=False)
                        t = mm(ob[:, 128:256], vT[:, 1, ec:ec + 128], AT[:, h % 2, 256:384], start=False, stop=True, mark=True)
                    src = b.t[:, :].rearrange("p (a b) -> p a b", b=256)
                    a1 = act.do(act_(o[:, 2 * pr:2 * pr + 2, :], src, ACT.Copy), t, ot.get((h - 1, "dve")))
                    b.rd.append(a1)
                    sq_ = act.do(act_(osq[:, 2 * pr:2 * pr + 2, :], o[:, 2 * pr:2 * pr + 2, :], ACT.Square), a1, ot.get((h - 1, "sum")))
                    ev.append(sq_)
                ot[h, "pe"] = t
                yield
                a = dve.do(tt_op(osq[:, 0:2, :], osq[:, 0:2, :], osq[:, 2:4, :], ALU.add), *ev)
                b = banks[5]
                pe.wait(b.take(), a)
                mm(b.t[:, 0:256], ones, osq[:, 0, :], start=True, stop=False)
                t = mm(b.t[:, 0:256], ones, osq[:, 1, :], start=False, stop=True, mark=True)
                ot[h, "sum"] = t
                r = rstd_of(b.t[:, 0:256], Ro[:, 1, :], epsc[:, 0:1], Ro[:, 0, :], [t, ot.get((h - 1, "dve"))], bank=b, scale=1.0 / 512)
                yield
                dst = hb[h % 2]
                res = []
                for e_ in range(4):
                    i = h * 4 + e_
                    a = dve.do(stt_op(
                        o[:, e_, :], o[:, e_, :], P("ron", i), Ro[:, 1, :], ALU.mult, ALU.mult), r)
                    a = dve.do(tt_op(o[:, e_, :], o[:, e_, :], sg[:, i, :], ALU.mult), a, gt[i])
                    res.append(split(o[:, e_, :], dst[0][:, e_, :], dst[1][:, e_, :], waits=[a, ows.get(h - 2)]))
                    if e_ == 1:
                        yield
                ot[h, "dve"] = [res[-1][0], res[-1][1]]
                ot[h] = res

            for i in range(16):
                b = banks[i % 4]
                t = gemm_fm("ow_g", i, b, 0, xh, xl)
                a = dve.do(tt_op(sg[:, i, :], b.t[:, 0:256], R[:, 0, :], ALU.mult), t)
                b.rd.append(a)
                gt[i] = act.do(act_(sg[:, i, :], sg[:, i, :], ACT.Silu), a)
                if i in (6, 12):
                    side.append(head(0 if i == 6 else 1))
                step()
            finish()
            for h in range(4):
                if h < 3 and (h + 1) not in ot:
                    side.append(head(h + 1))
                for k in range(4):
                    if k == 0 and h not in ot:
                        finish()
                    toks = gemm_acc("ow_out", h * 4 + k, hb[h % 2][0], hb[h % 2][1], k, h == 0 and k == 0, h == 3 and k == 3,
                                    waits=ot[h][k])
                    ows[h] = toks[-1]
                    step()
                finish()
            return toks

        def hybrid(l, xt):
            ar = Arena()
            fr = everyone()
            for q in (dve, act, pool):
                q.wait(*fr)
            qb, kb, vb = ar.get(4, 256), ar.get(4, 256), ar.get(2, 512)
            qc, kc, vc = ar.get(4, 256), ar.get(1, 256), ar.get(2, 128)
            S = ar.get(4, 384)
            PT = S
            bb = ar.get(4, 384)
            pre = ar.get(4, 256)
            cv = ar.get(12, 256)
            kT, vT = ar.get(8, 128), ar.get(8, 128)
            negd = ar.get(384)
            st = ar.get(5, 8)
            sm = ar.get(24, 8)
            zf = ar.get(4, 256)
            DT, nLT, AT, kbg, T, TT = (ar.get(8, 128) for _ in range(6))
            Y, U_, wT, S1 = DT, vT, nLT[:, 0:4, :], nLT[:, 4:8, :]
            mgs = [t1[:, 0:2, :], t1[:, 2:4, :], t2[:, 0:2, :], t2[:, 2:4, :]]
            chs = [chan(f"s_m{l}{i}") for i in range(3)]
            tb = [sp.dma(chs[0], rowc[:, 0:ROWC], ins[f"rowc{l}"].partition_broadcast(128), fr),
                  sp.dma(chs[1], bb, ins[f"relb{l}"], fr),
                  sp.dma(chs[2], negd, c[:, COFF["negd"]:COFF["negd"] + 384], fr)]
            ROW = {"vb": (0, 512), "vc": (512, 128), "ba": (640, 8), "al": (648, 4), "dt": (652, 4), "sk": (656, 8)}

            def row(n):
                return rowc[:, ROW[n][0]:ROW[n][0] + ROW[n][1]]

            qbt = []
            early = gemm_fm_first([(f"mw_qkb{l}", i, banks[i], 0) for i in range(4)], xh, xl, xt)
            for i in range(8):
                b = banks[i % 4]
                t = early[i] if i < 4 else gemm_fm(f"mw_qkb{l}", i, b, 0, xh, xl)
                dst, nm = (qb[:, i, :], "bqb") if i < 4 else (kb[:, i - 4, :], "bkb")
                a = act.do(act_(dst, b.t[:, 0:256], ACT.Identity, bias=P(f"{nm}{l}", i % 4)), t)
                b.rd.append(a)
                qbt.append(a)
            t = gemm_tm(f"mw_vb{l}", 0, [banks[2], banks[3]], xh, xl, 8, 2, 512)
            dve.wait(*tb)
            for tt in range(2):
                b = banks[2 + tt]
                a = dve.do(tt_op(vb[:, tt, :], b.t[:, :], row("vb"), ALU.add), t)
                b.rd.append(a)
                qbt.append(a)
            oB, oBt, oC, oCt = h1, {}, h2, {}

            def putB(h, pt, v, w):
                b = banks[2 + h % 2]
                pe.wait(b.take())
                t = pv(b.t[:, 0:256], pt, v, [w])
                oBt[h] = split(b.t[:, 0:256], oB[0][:, h, :], oB[1][:, h, :], waits=[t])
                b.rd += oBt[h]

            def putC(h, pt, v, w):
                j, g = h // 2, h % 2
                b = banks[2 + j % 2]
                if g == 0:
                    pe.wait(b.take())
                t = pv(b.t[64 * g:64 * g + 64, 0:256], pt, v, [w])
                if g == 1:
                    oCt[j] = split(b.t[:, 0:256], oC[0][:, j, :], oC[1][:, j, :], waits=[t])
                    b.rd += oCt[j]

            done = {}

            def both():
                yield from attend(4, lambda h: qb[:, h, :], lambda h: kb[:, h, :],
                                  lambda h: [vb[:, n, h * 128:h * 128 + 128] for n in range(2)],
                                  lambda h: bb[:, h, :], S, PT, st, [banks[2], banks[3]], putB, float(128 ** -0.5), ready=qbt)
                while "c" not in done:
                    yield

                def slope(h):
                    hh = (h % 2) * 4 + h // 2
                    return float(2.0 ** -(hh + 1))

                yield from attend(8, lambda h: qc[64 * (h % 2):64 * (h % 2) + 64, h // 2, :],
                                  lambda h: kc[64 * (h % 2):64 * (h % 2) + 64, 0, :],
                                  lambda h: [vc[:, n, 64 * (h % 2):64 * (h % 2) + 64] for n in range(2)],
                                  lambda h: negd, S, PT, st, [banks[2], banks[3]], putC, 1.0,
                                  sink=lambda h0: row("sk")[:, h0:h0 + 4], slope=slope, ready=done["c"])
                done["attn"] = everyone()

            side.append(both())
            ct = []
            for i in range(5):
                b = banks[i % 2]
                t = gemm_fm(f"mw_c{l}", i, b, 0, xh, xl)
                if i < 4:
                    a = dve.do(ts_op(qc[:, i, :], b.t[:, 0:256], P(f"bqc{l}", i), 0.125, ALU.add, ALU.mult), t)
                else:
                    a = dve.do(ts_op(kc[:, 0, :], b.t[:, 0:256], P(f"bkc{l}", 0), None, ALU.add), t)
                b.rd.append(a)
                ct.append(a)
                step()
            b = banks[2]
            t = gemm_tm(f"mw_c{l}", 5, [b], xh, xl, 8, 8, 128)
            a = dve.do(tt_op(vc, b.t[:, 0:256].rearrange("p (a b) -> p a b", b=128),
                                                 row("vc").unsqueeze(1).broadcast_to([128, 2, 128]), ALU.add), t)
            b.rd.append(a)
            ct.append(a)
            done["c"] = ct
            step()
            b = banks[3]
            t = gemm_tm(f"mw_ba{l}", 0, [b], xh, xl, 8, 8, 8)
            BA, BE, G, GC, KD, EG, W0, W1, W2, W3, EA, BG = (sm[:, 2 * i:2 * i + 2, :] for i in range(12))
            a = dve.do(tt_op(BA, b.t[:, 0:16].rearrange("p (a b) -> p a b", b=8),
                                                 row("ba").unsqueeze(1).broadcast_to([128, 2, 8]), ALU.add), t)
            b.rd.append(a)

            def f8(v):
                return v[:, 0, :]

            def f24(v):
                return v[:, 0, :].rearrange("p (n h) -> p n h", h=4)

            def small(t):
                dv = dve.do
                be = act.do(act_(f24(BE), BA[:, :, 0:4], ACT.Sigmoid), t)
                a = dv(tt_op(f24(W0), BA[:, :, 4:8], row("dt").unsqueeze(1).broadcast_to([128, 2, 4]), ALU.add), t)
                ea = act.do(act_(EA[:, 0, 0:4], row("al"), ACT.Exp), a, *tb)
                n = dv(ts_op(f8(W1), f8(W0), -1.0, None, ALU.mult), a)
                n = dv(tt_op(f8(W1), f8(W1), f8(W0), ALU.min), n)
                y = act.do(act_(f8(W1), f8(W1), ACT.Exp), n)
                yield
                s = dv(ts_op(f8(W2), f8(W1), 2.0, None, ALU.add), y)
                s = dv(rcp_op(f8(W3), f8(W2)), s)
                s = dv(tt_op(f8(W1), f8(W1), f8(W3), ALU.mult), s)
                s = dv(tt_op(f8(W2), f8(W1), f8(W1), ALU.mult), s)
                s = dv(ts_op(f8(W3), f8(W2), 2.0 / 17, 2.0 / 15, ALU.mult, ALU.add), s)
                for cf in (13, 11, 9, 7, 5, 3, 1):
                    s = dv(tt_op(f8(W3), f8(W3), f8(W2), ALU.mult), s)
                    s = dv(ts_op(f8(W3), f8(W3), 2.0 / cf, None, ALU.add), s)
                s = dv(tt_op(f8(W3), f8(W3), f8(W1), ALU.mult), s)
                yield
                s = dv(stt_op(f8(W3), f8(W0), 0.0, f8(W3), ALU.max, ALU.add), s)
                s = dv(stt_op(f24(G), f24(W3), -1.0, EA[:, 0:1, 0:4].broadcast_to([128, 2, 4]),
                                                        ALU.mult, ALU.mult), s, ea)
                b = banks[3]
                pe.wait(b.take(), s, tc)
                mm(b.t[:, 0:8], Ucum, f8(G))
                t = mm(b.t[:, 8:16], ones, f8(G), mark=True)
                a = dv(copy_op(f8(GC), b.t[:, 0:8]), t)
                k = dv(tt_op(f8(KD), b.t[:, 8:16], f8(GC), ALU.subtract), a)
                b.rd.append(k)
                k = act.do(act_(f8(KD), f8(KD), ACT.Exp), k)
                g = act.do(act_(f8(EG), f8(GC), ACT.Exp), a)
                done["sm"] = [dv(tt_op(f8(BG), f8(EG), f8(BE), ALU.mult), g, be), k]

            side.append(small(a))
            cvt = {}
            for i in range(12):
                b = banks[i % 2]
                t = gemm_fm(f"mw_a{l}", i, b, 0, xh, xl)
                pr = pre[:, i % 4, :]
                a = act.do(act_(pr, b.t[:, 0:256], ACT.Identity, bias=P(f"bqa{l}", i)), t, cvt.get(i - 4))
                b.rd.append(a)
                y = cv[:, i, :]
                a = dve.do(ts_op(y, pr, P(f"cw{l}", 36 + i), None, ALU.mult), a)
                for d in (1, 2, 3):
                    a = dve.do(stt_op(
                        y[:, d:256], pr[:, 0:256 - d], P(f"cw{l}", (3 - d) * 12 + i), y[:, d:256], ALU.mult, ALU.add), a)
                cvt[i] = act.do(act_(y, y, ACT.Silu), a)
                step()
            zt = []
            for i in range(4):
                b = banks[i % 2]
                t = gemm_fm(f"mw_z{l}", i, b, 0, xh, xl)
                a = act.do(act_(zf[:, i, :], b.t[:, 0:256], ACT.Silu, bias=P(f"bza{l}", i)), t)
                b.rd.append(a)
                zt.append(a)
                step()
            oAt = {}

            def delta():
                bk = banks[4:8]
                for p in range(4):
                    v = cv[:, 2 * p:2 * p + 2, :]
                    sq_ = pre[:, (p % 2) * 2:(p % 2) * 2 + 2, :]
                    a = act.do(act_(sq_, v, ACT.Square), cvt[2 * p], cvt[2 * p + 1], cvt[11], done.get(("n", p - 2)))
                    b = bk[p % 2]
                    pe.wait(b.take(), a)
                    t = mm(b.t[:, :], ones, sq_.rearrange("p a b -> p (a b)"), mark=True)
                    src = b.t[:, :].rearrange("p (a b) -> p a b", b=256)
                    a = act.do(act_(sq_, src, ACT.Sqrt, bias=epsc[:, 0:1]), t)
                    b.rd.append(a)
                    a = dve.do(rcp_op(sq_, sq_), a)
                    scl = float(128 ** -0.5) if p < 2 else 1.0
                    done["n", p] = dve.do(stt_op(v, v, scl, sq_, ALU.mult, ALU.mult), a)
                    if p % 2 == 1:
                        yield
                while "sm" not in done:
                    yield
                smt = done["sm"]
                q_, k_, v_ = cv[:, 0:4, :], cv[:, 4:8, :], cv[:, 8:12, :]
                nt = [done["n", p] for p in range(4)]
                kt, vt_, kg = [], [], []
                for n in range(2):
                    b, b2 = bk[2 * n], bk[2 * n + 1]
                    s4 = slice(4 * n, 4 * n + 4)
                    pe.wait(b.take(), *nt)
                    for h in range(4):
                        t = tr(b.t[:, h * 128:h * 128 + 128], k_[:, h, n * 128:n * 128 + 128], ident, mark=h == 3)
                    src = b.t[:, :].rearrange("p (a b) -> p a b", b=128)
                    a = act.do(act_(kT[:, s4, :], src, ACT.Copy), t)
                    b.rd.append(a)
                    pe.wait(b2.take(), *[cvt[8 + h] for h in range(4)])
                    for h in range(4):
                        t = tr(b2.t[:, h * 128:h * 128 + 128], v_[:, h, n * 128:n * 128 + 128], ident, mark=h == 3)
                    src = b2.t[:, :].rearrange("p (a b) -> p a b", b=128)
                    be = f8(BE)[:, s4].unsqueeze(2).broadcast_to([128, 4, 128])
                    v = dve.do(tt_op(vT[:, s4, :], src, be, ALU.mult), t, *smt)
                    b2.rd.append(v)
                    vt_.append(v)
                    bg = f8(BG)[:, s4].unsqueeze(2).broadcast_to([128, 4, 128])
                    kg.append(dve.do(tt_op(kbg[:, s4, :], kT[:, s4, :], bg, ALU.mult), a))
                    if n == 0:
                        kd = f8(KD)[:, s4].unsqueeze(2).broadcast_to([128, 4, 128])
                        kg.append(dve.do(tt_op(kT[:, s4, :], kT[:, s4, :], kd, ALU.mult), kg[-1]))
                    yield
                DG = T
                for n in range(2):
                    s4 = slice(4 * n, 4 * n + 4)
                    b, b2 = bk[2 * n], bk[2 * n + 1]
                    idb = ident.unsqueeze(1).broadcast_to([128, 4, 128])
                    a = dve.do(tt_op(
                        DG[:, s4, :], idb, f8(GC)[:, s4].unsqueeze(2).broadcast_to([128, 4, 128]), ALU.mult), *smt)
                    a2 = dve.do(tt_op(
                        TT[:, s4, :], idb, f8(BE)[:, s4].unsqueeze(2).broadcast_to([128, 4, 128]), ALU.mult), *smt)
                    pe.wait(b.take(), b2.take(), a, a2)
                    t = mm(b.t[:, :], ones, DG[:, s4, :].rearrange("p a b -> p (a b)"), mark=True)
                    t2_ = mm(b2.t[:, :], ones, TT[:, s4, :].rearrange("p a b -> p (a b)"), mark=True)
                    ds = []
                    for h in range(4):
                        s = 4 * n + h
                        ds.append(dve.do(stt_op(
                            DT[:, s, :], b.t[:, h * 128:h * 128 + 128], f8(GC)[:, s:s + 1], NEGU, ALU.subtract, ALU.add), t))
                    if n == 1:
                        src = b.t[:, :].rearrange("p (a b) -> p a b", b=128)
                        qe = act.do(act_(pre.rearrange("p a (b c) -> p (a b) c", c=128)[:, 0:4, :], src, ACT.Exp), ds[-1], *nt)
                        b.rd.append(qe)
                    b.rd.append(ds[-1])
                    dte = act.do(act_(DT[:, s4, :], DT[:, s4, :], ACT.Exp), *ds)
                    src2 = b2.t[:, :].rearrange("p (a b) -> p a b", b=128)
                    w = dve.do(tt_op(nLT[:, s4, :], DT[:, s4, :], src2, ALU.mult), dte, t2_)
                    b2.rd.append(w)
                    w = dve.do(tt_op(nLT[:, s4, :], nLT[:, s4, :],
                                                                nSU.unsqueeze(1).broadcast_to([128, 4, 128]), ALU.mult), w)
                    yield
                    pe.wait(b.take(), b2.take())
                    for h in range(4):
                        ks = k_[:, h, n * 128:n * 128 + 128]
                        mm(b.t[:, h * 128:h * 128 + 128], ks, ks)
                    for h in range(4):
                        ks = k_[:, h, n * 128:n * 128 + 128]
                        t = mm(b2.t[:, h * 128:h * 128 + 128], ks, q_[:, h, n * 128:n * 128 + 128], mark=True)
                    src = b.t[:, :].rearrange("p (a b) -> p a b", b=128)
                    l_ = dve.do(tt_op(nLT[:, s4, :], nLT[:, s4, :], src, ALU.mult), t, w)
                    b.rd.append(l_)
                    at = dve.do(tt_op(AT[:, s4, :], DT[:, s4, :], src2, ALU.mult), t)
                    b2.rd.append(at)
                    done["L", n] = l_
                    done["AT", n] = at
                    yield
                qd = dve.do(tt_op(pre.rearrange("p a (b c) -> p (a b) c", c=128)[:, 0:4, :],
                                                      pre.rearrange("p a (b c) -> p (a b) c", c=128)[:, 0:4, :],
                                                      q_[:, :, 128:256], ALU.mult), qe, *nt)
                tt, ttt = {}, {}
                for n in range(2):
                    s4 = slice(4 * n, 4 * n + 4)
                    idb = ident.unsqueeze(1).broadcast_to([128, 4, 128])
                    b = bk[n]
                    pe.wait(b.take(), done["L", n])
                    for h in range(4):
                        t = tr(b.t[:, h * 128:h * 128 + 128], nLT[:, 4 * n + h, :], ident, mark=h == 3)
                    i1 = pool.do(copy_op(T[:, s4, :], idb), done["AT", 1], t, apos_pe[0])
                    i2 = pool.do(copy_op(TT[:, s4, :], idb), done["AT", 1])
                    src = b.t[:, :].rearrange("p (a b) -> p a b", b=128)
                    tt[n] = dve.do(pred_op(
                        T[:, s4, :], lvm[:, 0:1, :].broadcast_to([128, 4, 128]), src), t, i1, tl)
                    b.rd.append(tt[n])
                    ttt[n] = dve.do(pred_op(
                        TT[:, s4, :], lvm[:, 7:8, :].broadcast_to([128, 4, 128]), nLT[:, s4, :]), i2, tt[n])
                yield
                for lv in range(1, 7):
                    yt_ = {}
                    for n in range(2):
                        s4 = slice(4 * n, 4 * n + 4)
                        b = bk[n]
                        pe.wait(b.take(), tt[n], ttt[n])
                        for h in range(4):
                            s = 4 * n + h
                            t = mm(b.t[:, h * 128:h * 128 + 128], nLT[:, s, :], T[:, s, :], mark=h == 3)
                        src = b.t[:, :].rearrange("p (a b) -> p a b", b=128)
                        yt_[n] = act.do(act_(Y[:, s4, :], src, ACT.Copy), t)
                        b.rd.append(yt_[n])
                    yield
                    for n in range(2):
                        s4 = slice(4 * n, 4 * n + 4)
                        b, b2 = bk[2], bk[3]
                        pe.wait(yt_[n])
                        if lv < 6:
                            pe.wait(b.take())
                            for h in range(4):
                                s = 4 * n + h
                                t = mm(b.t[:, h * 128:h * 128 + 128], TT[:, s, :], Y[:, s, :], mark=h == 3)
                        pe.wait(b2.take())
                        for h in range(4):
                            s = 4 * n + h
                            t2_ = mm(b2.t[:, h * 128:h * 128 + 128], Y[:, s, :], TT[:, s, :], mark=h == 3)
                        if lv < 6:
                            src = b.t[:, :].rearrange("p (a b) -> p a b", b=128)
                            tt[n] = dve.do(pred_op(
                                T[:, s4, :], lvm[:, lv:lv + 1, :].broadcast_to([128, 4, 128]), src), t2_)
                            b.rd.append(tt[n])
                        src2 = b2.t[:, :].rearrange("p (a b) -> p a b", b=128)
                        ttt[n] = dve.do(pred_op(
                            TT[:, s4, :], lvm[:, 7 + lv:8 + lv, :].broadcast_to([128, 4, 128]), src2), t2_)
                        b2.rd.append(ttt[n])
                        yield
                ut = []
                for n in range(2):
                    b = bk[n]
                    pe.wait(b.take(), ttt[n], *vt_, *kg)
                    for h in range(4):
                        s = 4 * n + h
                        t = mm(b.t[:, h * 128:h * 128 + 128], TT[:, s, :], vT[:, s, :], mark=h == 3)
                    src = b.t[:, :].rearrange("p (a b) -> p a b", b=128)
                    ut.append(act.do(act_(U_[:, 4 * n:4 * n + 4, :], src, ACT.Copy), t))
                    b.rd.append(ut[-1])
                b = bk[2]
                pe.wait(b.take())
                for h in range(4):
                    t = mm(b.t[:, h * 128:h * 128 + 128], kbg[:, 4 + h, :], TT[:, 4 + h, :], mark=h == 3)
                src = b.t[:, :].rearrange("p (a b) -> p a b", b=128)
                wt_ = act.do(act_(wT, src, ACT.Copy), t)
                b.rd.append(wt_)
                yield
                b = bk[3]
                pe.wait(b.take(), ut[0], *kg)
                for h in range(4):
                    t = mm(b.t[:, h * 128:h * 128 + 128], kT[:, h, :], U_[:, h, :], mark=h == 3)
                src = b.t[:, :].rearrange("p (a b) -> p a b", b=128)
                s1 = act.do(act_(S1, src, ACT.Copy), t)
                b.rd.append(s1)
                b = bk[0]
                pe.wait(b.take(), done["AT", 0])
                for h in range(4):
                    t = mm(b.t[:, h * 128:h * 128 + 128], U_[:, h, :], AT[:, h, :], mark=h == 3)
                o_ = cv[:, 8:12, :]
                src0 = b.t[:, :].rearrange("p (a b) -> p a b", b=128)
                o0 = act.do(act_(o_[:, :, 0:128], src0, ACT.Copy), t)
                b.rd.append(o0)
                yield
                b = bk[1]
                pe.wait(b.take(), s1, wt_)
                for h in range(4):
                    t = mm(b.t[:, h * 128:h * 128 + 128], wT[:, h, :], S1[:, h, :], mark=h == 3)
                src = b.t[:, :].rearrange("p (a b) -> p a b", b=128)
                vn = dve.do(tt_op(U_[:, 4:8, :], U_[:, 4:8, :], src, ALU.subtract), t, ut[1])
                b.rd.append(vn)
                yield
                b = bk[2]
                pe.wait(b.take(), vn, qd, done["AT", 1])
                for h in range(4):
                    o = b.t[:, h * 128:h * 128 + 128]
                    mm(o, S1[:, h, :], pre.rearrange("p a (b c) -> p (a b) c", c=128)[:, h, :], start=True, stop=False)
                    t = mm(o, U_[:, 4 + h, :], AT[:, 4 + h, :], start=False, stop=True, mark=h == 3)
                src = b.t[:, :].rearrange("p (a b) -> p a b", b=128)
                o1 = act.do(act_(o_[:, :, 128:256], src, ACT.Copy), t)
                b.rd.append(o1)
                yield
                for p in range(2):
                    v = o_[:, 2 * p:2 * p + 2, :]
                    sq_ = Y.rearrange("p (a b) c -> p a (b c)", b=2)[:, 2 * p:2 * p + 2, :]
                    a = act.do(act_(sq_, v, ACT.Square), o0, o1)
                    b = bk[p]
                    pe.wait(b.take(), a)
                    t = mm(b.t[:, :], ones, sq_.rearrange("p a b -> p (a b)"), mark=True)
                    src = b.t[:, :].rearrange("p (a b) -> p a b", b=256)
                    a = act.do(act_(sq_, src, ACT.Sqrt, bias=epsc[:, 0:1], scale=1.0 / 128), t)
                    b.rd.append(a)
                    a = dve.do(rcp_op(sq_, sq_), a)
                    a = dve.do(stt_op(v, v, P(f"gng{l}"), sq_, ALU.mult, ALU.mult), a)
                    a = dve.do(tt_op(v, v, zf[:, 2 * p:2 * p + 2, :], ALU.mult), a, *zt)
                    yield
                    for k in (2 * p, 2 * p + 1):
                        oAt[k] = split(o_[:, k, :], h1[0][:, k, :], h1[1][:, k, :], waits=[a, done["brb"]])
                done["A"] = 1

            side.append(delta())
            mt = {}

            def branch(br, oh, ot, waits_for):
                last = None
                for p in range(4):
                    bg, bo = banks[0], banks[1]
                    gemm_fm(f"mw_g{l}", br * 8 + 2 * p, bg, 0, xh, xl)
                    step()
                    t = gemm_fm(f"mw_g{l}", br * 8 + 2 * p + 1, bg, 1, xh, xl)
                    g = gt2[:, :, :]
                    gs = []
                    for i in range(2):
                        gs.append(act.do(act_(
                            g[:, i, :], bg.t[:, i * 256:i * 256 + 256], ACT.Sigmoid, bias=P(f"bg{l}", br * 8 + 2 * p + i)), t, mt.get("g")))
                    bg.rd.append(gs[-1])
                    step()
                    waits_for()
                    wv = ws.next(f"mw_br{l}", br * 4 + p)
                    pe.wait(bo.take())
                    for i in range(2):
                        o = bo.t[:, i * 256:i * 256 + 256]
                        for k in range(4):
                            pe.wait(*ot[k])
                            co = (i * 4 + k) * 128
                            t = mm3(o, wv[0][:, co:co + 128], wv[1][:, co:co + 128], oh[0][:, k, :], oh[1][:, k, :],
                                    k == 0, k == 3, None, i == 1 and k == 3)
                    ws.done(t)
                    last = t
                    m = mgs[p]
                    src = bo.t[:, :].rearrange("p (a b) -> p a b", b=256)
                    if br == 1:
                        a = dve.do(tt_op(m, g, src, ALU.mult), t, *gs)
                        bo.rd.append(a)
                        mt["g"] = a
                    else:
                        a = dve.do(tt_op(g, g, src, ALU.mult), t, *gs)
                        bo.rd.append(a)
                        a = dve.do(tt_op(m, m, g, ALU.add), a, mt[p])
                        mt["g"] = a
                    mt[p] = a
                    step()
                return last

            gt2 = R

            def until(key):
                def f():
                    while key not in done:
                        assert side
                        step()
                return f

            done["brb"] = branch(1, oB, oBt, until("attn"))
            branch(2, oC, oCt, until("attn"))
            lastg = branch(0, h1, oAt, until("A"))
            finish()
            sp2 = []
            for k in range(8):
                sp2.append(split(mgs[k // 2][:, k % 2, :], xh[:, k, :], xl[:, k, :], waits=[mt[k // 2], lastg]))
            for k in range(8):
                toks = gemm_acc(f"mw_o{l}", k, xh, xl, k, k == 0, k == 7, waits=sp2[k])
            return toks

        phase = [0]

        def ended():
            phase[0] += 1
            return phase[0] >= stop

        def plain(toks):
            return [[add_pair(p, toks[p], 1.0)] for p in range(4)]

        def body(xt):
            toks = even(xt)
            if ended():
                return plain(toks)
            for i in range(2):
                if i:
                    toks = odd(toks)
                    if ended():
                        return plain(toks)
                pt, sq_, _ = rms_parts(f"nf{i}", toks)
                toks = ffn(f"fg{i}", f"fu{i}", f"fd{i}", 22, pt, stats=lambda: rms_stats(sq_, nxt=ACT.Silu))
                if ended():
                    return plain(toks)
            xs, _, _ = rms_parts(None, toks)
            for l in range(2):
                for f in range(2):
                    toks = ffn(f"sg{f}{l}", f"su{f}{l}", f"sd{f}{l}", 32, xs, half=0.5)
                    dve.wait(xready[0])
                    fin = l == 1 and f == 1
                    xs = layer_norm(f"l{2 * f + 1}g{l}", f"l{2 * f + 1}b{l}", toks, final=fin)
                    if ended() or fin:
                        return xs + [[xready[0]]]
                    if f == 0:
                        toks = hybrid(l, xs)
                        dve.wait(xready[0])
                        xs = layer_norm(f"l2g{l}", f"l2b{l}", toks)
                        if ended():
                            return xs + [[xready[0]]]

        xt = body(xt)
        fr = everyone()
        otm = arena[:, 0:2048].rearrange("p (a b) -> p a b", b=1024)
        ot = []
        for tt in range(2):
            for hf in range(2):
                b = banks[4 + tt * 2 + hf]
                pe.wait(b.take(), *[z for y in xt for z in y], fr)
                for k in range(4):
                    t = tr(b.t[:, k * 128:k * 128 + 128], x[:, hf * 4 + k, tt * 128:tt * 128 + 128], ident, mark=k == 3)
                dst = otm[:, tt, hf * 512:hf * 512 + 512]
                q = act if hf else dve
                if hf:
                    a = act.do(act_(dst, b.t[:, :], ACT.Copy), t, fr)
                else:
                    a = dve.do(copy_op(dst, b.t[:, :]), t, fr)
                ot.append(a)
            o = out[tt * 128:tt * 128 + 128, :]
            sp.dma(s_out, o, otm[:, tt, :], *ot)
        sp.wait((s_out, s_out.n))
        if dry:
            return apos[0]

        block = ctx.enter_context(nc.Block())

        @block.sync
        def _(e):
            for f in sp.items:
                f(e)

        @block.scalar
        def _(e):
            for f in act.items:
                f(e)

        @block.vector
        def _(e):
            for f in dve.items:
                f(e)

        @block.gpsimd
        def _(e):
            for f in pool.items:
                f(e)

        @block.tensor
        def _(e):
            for f in pe.items:
                f(e)
        return apos[0]


def fm(w):
    K, N = w.shape
    return w.reshape(K // 128, 128, N // 128, 128).transpose(2, 1, 0, 3).reshape(N // 128, 128, K)


def tm(w, kper, n):
    K, N = w.shape
    return w.reshape(K // (kper * 128), kper, 128, N // n, n).transpose(3, 0, 2, 1, 4).reshape(-1, 128, kper * n)


def cols(v):
    return v.reshape(-1, 128).T


def lay_out(a):
    d = {}
    w = a["even_w_in"][0]
    d["ew_c"] = fm(w[:, 1024:1664])
    d["ew_pe"] = tm(w[:, 1664:1696], 8, 32)
    d["ew_u"] = fm(w[:, 0:512])
    d["ew_v"] = tm(w[:, 512:1024], 2, 512)
    d["ew_ukv"] = tm(a["mla_w_ukv"][0], 2, 512)
    d["ew_uq"] = tm(a["mla_w_uq"][0], 3, 256)
    d["ew_out"] = a["even_w_out"][0].reshape(8, 128, 1024)
    w = a["odd_w_in"][0]
    d["ow_v"] = tm(w[:, 2048:4096], 2, 512)
    qk = fm(w[:, 0:2048]).reshape(2, 4, 2, 128, 1024)
    d["ow_qk"] = qk.transpose(1, 0, 2, 3, 4).reshape(16, 128, 1024)
    d["ow_g"] = fm(w[:, 4096:6144])
    d["ow_out"] = a["odd_w_out"][0].reshape(16, 128, 1024)
    for i in range(2):
        d[f"fg{i}"] = fm(a["ffn_w_gate"][i])
        d[f"fu{i}"] = fm(a["ffn_w_up"][i])
        d[f"fd{i}"] = a["ffn_w_down"][i].reshape(22, 128, 1024)
    pk = [cols(a["norm_mix"][0]), cols(a["norm_mix"][1]), cols(a["norm_ffn"][0]), cols(a["norm_ffn"][1]),
          cols(a["gm_v_norm"][0]), cols(a["mla_q_a_norm"][0]), cols(a["mla_kv_a_norm"][0]), cols(a["ret_out_norm"][0])]
    qperm = np.concatenate([np.r_[j * 64:j * 64 + 64, (4 + j) * 64:(4 + j) * 64 + 64] for j in range(4)])
    hperm = [0, 4, 1, 5, 2, 6, 3, 7]
    own = np.arange(128)[None, :] // 64 <= np.arange(128)[:, None] // 64
    for l in range(2):
        for f in range(2):
            w = a[f"w_ff{f + 1}_in_2"][l]
            d[f"sg{f}{l}"] = fm(w[:, 0:4096])
            d[f"su{f}{l}"] = fm(w[:, 4096:8192])
            d[f"sd{f}{l}"] = a[f"w_ff{f + 1}_out_2"][l].reshape(32, 128, 1024)
        w, b = a["w_in_2"][l], a["b_in_2"][l]
        d[f"mw_qkb{l}"] = fm(w[:, 2056:3080])
        d[f"mw_vb{l}"] = tm(w[:, 3080:3592], 2, 512)
        qc = w[:, 3592:4104][:, qperm]
        d[f"mw_c{l}"] = np.concatenate([fm(np.concatenate([qc, w[:, 4104:4232]], 1)), tm(w[:, 4232:4360], 8, 128)])
        d[f"mw_ba{l}"] = tm(w[:, 1536:1544], 8, 8)
        d[f"mw_a{l}"] = fm(w[:, 0:1536])
        d[f"mw_z{l}"] = fm(w[:, 1544:2056])
        d[f"mw_g{l}"] = fm(a["w_gate_2"][l])
        brs = [a["w_br_a_2"][l], a["w_br_b_2"][l], a["w_br_c_2"][l][qperm]]
        d[f"mw_br{l}"] = np.concatenate(
            [v.reshape(4, 128, 4, 2, 128).transpose(2, 1, 3, 0, 4).reshape(4, 128, 1024) for v in brs])
        d[f"mw_o{l}"] = a["w_out_2"][l].reshape(8, 128, 1024)
        d[f"rowc{l}"] = np.concatenate([b[3080:3592], b[4232:4360], b[1536:1544], a["a_log_2"][l], a["dt_bias_2"][l],
                                        a["sinks_2"][l][hperm]])
        q, m = np.arange(128)[:, None], np.arange(256)[None, :]
        idx = np.clip(128 + q - m, -63, 128) + 63
        rb = a["rel_bias_2"][l][:, idx]
        rb[:, :, 128:] = np.where(own[None], rb[:, :, 128:], np.float32(NEG))
        d[f"relb{l}"] = np.concatenate([rb[:, :, 128:], rb], 2).transpose(1, 0, 2)
        pk += [cols(a[n][l]) for n in ("ln1_g_2", "ln1_b_2", "ln2_g_2", "ln2_b_2", "ln3_g_2", "ln3_b_2")]
        pk += [cols(b[0:1536]), cols(b[1544:2056]), cols(b[2056:2568]), cols(b[2568:3080]), cols(b[3592:4104][qperm]),
               cols(b[4104:4232]), cols(a["b_gate_2"][l]), cols(a["conv_w_2"][l]), cols(a["gdn_norm_g_2"][l])]
    d["pack"] = np.concatenate(pk, 1)
    d["rowa"] = np.concatenate([a["mla_q_norm"][0], a["mla_k_norm"][0], a["gm_b_s"][0].reshape(-1)])
    d["gmw"] = a["gm_w_s"][0]
    d["x"] = a["x"][0]
    return d


def constants():
    f = np.float32
    i = np.arange(128)
    c = {"ident": np.eye(128), "ones": np.ones((128, 128)), "U": i[:, None] <= i[None, :],
         "nSU": -(i[:, None] < i[None, :]).astype(f), "NEGU": np.where(i[:, None] <= i[None, :], 0.0, NEG)}
    own = np.where(i[None, :] // 64 <= i[:, None] // 64, 0.0, NEG)
    c["mask"] = np.concatenate([own, np.zeros((128, 128)), own], 1)
    dist = 128 + i[:, None] - np.arange(256)[None, :]
    qch, kch = 2 + i[:, None] // 64, np.arange(256)[None, :] // 64
    nd = np.where((kch <= qch) & (kch >= qch - 2), -np.abs(dist), NEG)
    c["negd"] = np.concatenate([nd[:, 128:], nd], 1)
    inv = (f(10000.0) ** (-np.arange(128, dtype=f) / f(128))).astype(f)
    ang = (np.arange(256, dtype=f)[None, :] * inv[:, None]).astype(f)
    co, si = np.cos(ang), np.sin(ang)
    c["cc"] = np.concatenate([co, co], 1)
    c["ss"] = np.concatenate([-si, si], 1)
    lg = np.log(1.0 - 2.0 ** (-5.0 - np.arange(4)))
    dd = np.arange(256)[None, None, :] - i[:, None, None]
    c["dtr"] = np.where(dd >= 0, np.exp(lg[None, :, None] * np.maximum(dd, 0)), 0.0).reshape(128, 1024)
    inv = (f(10000.0) ** (-np.arange(16, dtype=f) / f(16))).astype(f)
    ang = (np.arange(256, dtype=f)[:, None] * inv[None, :]).astype(f).reshape(2, 128, 16).transpose(1, 0, 2).reshape(128, 32)
    c["cosT"], c["sinT"] = np.cos(ang), np.sin(ang)
    out = np.concatenate([np.asarray(c[n], f).reshape(128, w) for n, w in CONSTS], 1)
    lv = np.zeros((128, 14, 128), f)
    for k in range(7):
        bi, bj = i[:, None] >> k, i[None, :] >> k
        m = (bi % 2 == 1) & (bj == bi - 1)
        lv[:, k, :] = m
        lv[:, 7 + k, :] = m.T
    return out, lv


STOP = 99


def kernel(**inputs):
    import concourse.bacc as _bacc
    from concourse import mybir as _mybir
    from concourse.bass_utils import run_bass_kernel_spmd as _run

    a = {k: np.asarray(v) for k, v in inputs.items()}
    arrays = lay_out(a)
    arrays["consts"], arrays["lvmask"] = constants()
    arrays = {f"in_{k}": np.ascontiguousarray(v) for k, v in arrays.items()}

    def build(order, dry):
        nc = _bacc.Bacc("TRN2", target_bir_lowering=False, num_devices=1)
        ins = {k[3:]: nc.dram_tensor(k, v.shape, _mybir.dt.from_np(v.dtype), kind="ExternalInput").ap()
               for k, v in arrays.items()}
        out = nc.dram_tensor("out_0_dram", (256, 1024), F32, kind="ExternalOutput").ap()
        emit(nc, ins, out, STOP, order, dry)
        return nc

    order = []
    build(order, True)
    nc = build(order, False)
    r = _run(nc, [arrays], core_ids=[0])
    return r.results[0]["out_0_dram"].reshape(1, 256, 1024)
```

```python
from contextlib import ExitStack

import concourse.bass as bass
from concourse import mybir
import numpy as np

F32 = mybir.dt.float32
F32R = mybir.dt.float32r
U8 = mybir.dt.uint8
ALU = mybir.AluOpType
ACT = mybir.ActivationFunctionType
AX = mybir.AxisListType.X

NRAW, NHL, CW = 6, 5, 1024
ALPHA = float(4.0 ** 0.25)
NEG = -1e30
SQ2PI = float(np.sqrt(2.0 / np.pi))

PACK = [("nm0", 8), ("nm1", 8), ("nf0", 8), ("nf1", 8), ("gmv", 4), ("qan", 3), ("kvan", 2), ("ron", 16)]
for _l in range(2):
    PACK += [(f"l1g{_l}", 8), (f"l1b{_l}", 8), (f"l2g{_l}", 8), (f"l2b{_l}", 8), (f"l3g{_l}", 8), (f"l3b{_l}", 8),
             (f"bqa{_l}", 12), (f"bza{_l}", 4), (f"bqb{_l}", 4), (f"bkb{_l}", 4), (f"bqc{_l}", 4), (f"bkc{_l}", 1),
             (f"bg{_l}", 24), (f"cw{_l}", 48), (f"gng{_l}", 1)]
OFF, _n = {}, 0
for _name, _w in PACK:
    OFF[_name] = _n
    _n += _w
NPACK = _n
CONSTS = [("ident", 128), ("ones", 128), ("U", 128), ("nSU", 128), ("NEGU", 128), ("mask", 384), ("negd", 384),
          ("cc", 512), ("ss", 512), ("dtr", 1024), ("cosT", 32), ("sinT", 32)]
COFF, _n = {}, 0
for _name, _w in CONSTS:
    COFF[_name] = _n
    _n += _w
NCONST = _n
ROWC = 664


def act_(*a, **k):
    return lambda e: e.activation(*a, **k)


def tt_op(*a, **k):
    return lambda e: e.tensor_tensor(*a, **k)


def ts_op(*a, **k):
    return lambda e: e.tensor_scalar(*a, **k)


def stt_op(*a, **k):
    return lambda e: e.scalar_tensor_tensor(*a, **k)


def red_op(*a, **k):
    return lambda e: e.tensor_reduce(*a, **k)


def copy_op(*a, **k):
    return lambda e: e.tensor_copy(*a, **k)


def pred_op(*a, **k):
    return lambda e: e.copy_predicated(*a, **k)


def rcp_op(*a, **k):
    return lambda e: e.reciprocal(*a, **k)


def set_op(*a, **k):
    return lambda e: e.memset(*a, **k)


class Ch:

    def __init__(self, sem):
        self.sem, self.n = sem, 0


class Queue:

    def __init__(self, ch):
        self.items, self.seen, self.ch = [], {}, ch

    def wait(self, *tokens):
        for t in tokens:
            if t is None:
                continue
            if isinstance(t, list):
                self.wait(*t)
                continue
            ch, v = t
            if self.seen.get(id(ch), 0) < v:
                self.seen[id(ch)] = v
                self.items.append(lambda e, ch=ch, v=v: e.wait_ge(ch.sem, v))

    def do(self, fn, *tokens):
        self.wait(*tokens)
        ch = self.ch
        ch.n += 1
        self.items.append(lambda e: fn(e).then_inc(ch.sem, 1))
        return (ch, ch.n)

    def quiet(self, fn, *tokens):
        self.wait(*tokens)
        self.items.append(fn)

    def dma(self, ch, out, in_, *tokens):
        self.wait(*tokens)
        ch.n += 16
        self.items.append(lambda e: e.dma_start(out, in_).then_inc(ch.sem, 16))
        return (ch, ch.n)

    def last(self):
        return (self.ch, self.ch.n) if self.ch.n else None


class Bank:

    def __init__(self, t):
        self.t, self.rd = t, []

    def take(self):
        r, self.rd = self.rd, []
        return r


def emit(nc, ins, out, stop, order, dry):
    ctx = ExitStack()
    with ctx:
        def sb(name, shape, dt=F32):
            return ctx.enter_context(nc.sbuf_tensor(name, shape, dt))

        def chan(name):
            return Ch(ctx.enter_context(nc.semaphore(name)))

        raw = sb("raw", [128, NRAW, CW])
        whi = sb("whi", [128, NHL, CW], F32R)
        wlo = sb("wlo", [128, NHL, CW], F32R)
        x = sb("x", [128, 8, 256])
        xh = sb("xh", [128, 8, 256], F32R)
        xl = sb("xl", [128, 8, 256], F32R)
        h1 = [sb("h1h", [128, 4, 256], F32R), sb("h1l", [128, 4, 256], F32R)]
        h2 = [sb("h2h", [128, 4, 256], F32R), sb("h2l", [128, 4, 256], F32R)]
        t1 = sb("t1", [128, 4, 256])
        t2 = sb("t2", [128, 4, 256])
        R = sb("R", [128, 2, 256])
        pk = sb("pk", [128, NPACK])
        cst = sb("cst", [128, 640])
        lvm = sb("lvm", [128, 14, 128], U8)
        rowc = sb("rowc", [128, 704])
        epsc = sb("epsc", [128, 4])
        junk = sb("junk", [128, 1])[:, :]
        onm = sb("onm", [128, 128])[:, :]
        NAR = (nc.sbuf_bytes_remaining if not callable(nc.sbuf_bytes_remaining) else nc.sbuf_bytes_remaining()) // 4 - 64
        arena = sb("arena", [128, NAR])
        banks = [Bank(ctx.enter_context(nc.psum_tensor(f"ps{i}", [128, 512], F32))) for i in range(8)]

        ident, ones = cst[:, 0:128], cst[:, 128:256]
        Ucum, nSU, NEGU = cst[:, 256:384], cst[:, 384:512], cst[:, 512:640]

        pe, act, dve, pool, sp = (Queue(chan(f"s_{n}")) for n in ("pe", "act", "dve", "pool", "sp"))
        s_raw = [chan(f"s_raw{i}") for i in range(NRAW)]
        s_c = [chan(f"s_c{i}") for i in range(4)]
        s_tab = chan("s_tab")
        s_out = chan("s_out")

        apos = [0, 0]

        class Arena:

            def __init__(self):
                self.at = 0

            def get(self, *shape):
                n = int(np.prod(shape))
                v = arena[:, self.at:self.at + n]
                self.at += n
                apos[0] = max(apos[0], self.at)
                assert self.at <= NAR, (self.at, NAR)
                if len(shape) == 2:
                    v = v.rearrange("p (a b) -> p a b", b=shape[1])
                if len(shape) == 3:
                    v = v.rearrange("p (a b c) -> p a b c", b=shape[1], c=shape[2])
                return v

        def everyone():
            return [q.last() for q in (act, dve, pool)] + [apos_pe[0]]

        apos_pe = [None]

        def P(name, i=0, n=1):
            return pk[:, OFF[name] + i:OFF[name] + i + n]

        class Stream:
            def __init__(self):
                self.used, self.prepped, self.loaded, self.ndone = 0, 0, 0, 0
                self.hi_t, self.lo_t, self.raw_t, self.pe_t = {}, {}, {}, {}

            def load(self, upto):
                while self.loaded < min(upto, len(order)):
                    c = self.loaded
                    name, i = order[c]
                    src = ins[name]
                    w = src.shape[2]
                    prev = c - NRAW
                    self.raw_t[c] = sp.dma(s_raw[c % NRAW], raw[:, c % NRAW, 0:w], src[i],
                                           self.hi_t.get(prev), self.lo_t.get(prev))
                    self.loaded += 1

            def prep(self, upto):
                while self.prepped < min(upto, len(order)):
                    c = self.prepped
                    w = ins[order[c][0]].shape[2]
                    self.load(c + 1)
                    s, r = c % NHL, c % NRAW
                    self.hi_t[c] = act.do(act_(whi[:, s, 0:w], raw[:, r, 0:w], ACT.Copy),
                                          self.raw_t[c], self.pe_t.get(c - NHL))
                    self.lo_t[c] = dve.do(tt_op(
                        wlo[:, s, 0:w], raw[:, r, 0:w], whi[:, s, 0:w].bitcast(F32), ALU.subtract),
                        self.hi_t[c])
                    self.prepped += 1

            def next(self, name, i):
                c = self.used
                self.used += 1
                if dry:
                    order.append((name, i))
                    return whi[:, 0, :], wlo[:, 0, :]
                assert order[c] == (name, i)
                self.prep(self.ndone + NHL)
                self.load(self.ndone + NHL + NRAW)
                pe.wait(self.hi_t[c], self.lo_t[c])
                return whi[:, c % NHL, :], wlo[:, c % NHL, :]

            def done(self, tok, c=None):
                self.pe_t[self.used - 1 if c is None else c] = tok
                self.ndone += 1

        ws = Stream()
        side = []

        def step():
            for g in list(side):
                if next(g, "end") == "end":
                    side.remove(g)

        def finish():
            while side:
                step()

        def mm(out, lhsT, rhs, start=True, stop=True, mark=False, waits=()):
            def fn(e):
                return e.matmul(out, lhsT, rhs, start=start, stop=stop, skip_group_check=True)
            if mark:
                apos_pe[0] = pe.do(fn, *waits)
                return apos_pe[0]
            pe.quiet(fn, *waits)

        def tr(out, in_, idn, mark=False, waits=()):
            def fn(e):
                return e.transpose(out, in_, idn)
            if mark:
                apos_pe[0] = pe.do(fn, *waits)
                return apos_pe[0]
            pe.quiet(fn, *waits)

        def mm3(out, wh, wl, ah, al, start, stop, first, mark):
            mm(out, wh, ah, start=start, stop=False)
            mm(out, wl, ah, start=False, stop=False)
            return mm(out, wh, al, start=False, stop=stop, mark=mark)

        def gemm_fm(name, i, bank, half, ah, al, K=8, woff=0, fetch=True, wv=None, waits=(), first=None):
            if wv is None:
                wv = ws.next(name, i)
            wh, wl = wv
            o = bank.t[:, half * 256:half * 256 + 256]
            pe.wait(bank.take(), *waits)
            for k in range(K):
                c = woff + k * 128
                t = mm3(o, wh[:, c:c + 128], wl[:, c:c + 128], ah[:, k, :], al[:, k, :],
                        k == 0, k == K - 1, None, k == K - 1)
            ws.done(t)
            return t

        def gemm_fm_first(specs, ah, al, wk):
            c0 = ws.used
            wv = []
            toks = []
            for n, i, bank, half in specs:
                pe.wait(bank.take())
            for k in range(8):
                pe.wait(*wk[k])
                for m, (n, i, bank, half) in enumerate(specs):
                    c = k * 128
                    if k == 0:
                        wv.append(ws.next(n, i))
                    t = mm3(bank.t[:, half * 256:half * 256 + 256], wv[m][0][:, c:c + 128], wv[m][1][:, c:c + 128],
                            ah[:, k, :], al[:, k, :], k == 0 and half == 0, k == 7, None, k == 7)
                    if k == 7:
                        toks.append(t)
                        ws.done(t, c0 + m)
            ws.prep(ws.ndone + NHL)
            return toks

        def gemm_tm(name, i0, bks, ah, al, K, kper, n, woff=0, waits=(), col=0, after=None, wk=None):
            for b in bks:
                pe.wait(b.take())
            pe.wait(*waits)
            for c in range(K // kper):
                wh, wl = ws.next(name, i0 + c)
                for kk in range(kper):
                    k = c * kper + kk
                    if wk is not None:
                        pe.wait(*wk[k])
                    w0 = woff + kk * n
                    for tt in range(2):
                        b = bks[tt % len(bks)]
                        co = col + (n * tt if len(bks) == 1 else 0)
                        o = b.t[:, co:co + n]
                        s = slice(tt * 128, tt * 128 + 128)
                        st = k == 0
                        mm(o, ah[:, k, s], wh[:, w0:w0 + n], start=st and (len(bks) == 2 or tt == 0), stop=False)
                        mm(o, al[:, k, s], wh[:, w0:w0 + n], start=False, stop=False)
                        t = mm(o, ah[:, k, s], wl[:, w0:w0 + n], start=False, stop=k == K - 1,
                               mark=kk == kper - 1 and tt == 1)
                ws.done(t)
                if after:
                    after()
            return t

        def gemm_acc(name, i, ah, al, k, first, last, waits=(), kk=None):
            wh, wl = ws.next(name, i)
            pe.wait(*waits)
            toks = []
            for n in range(8):
                b = banks[n // 2]
                if first and n % 2 == 0:
                    pe.wait(b.take())
                o = b.t[:, (n % 2) * 256:(n % 2) * 256 + 256]
                t = mm3(o, wh[:, n * 128:n * 128 + 128], wl[:, n * 128:n * 128 + 128], ah[:, k, :], al[:, k, :],
                        first and n % 2 == 0, last, None, n == 7 or (last and n % 2 == 1))
                if n % 2 == 1:
                    toks.append(t)
            ws.done(t)
            return toks

        def split(src, dh, dl, g=None, waits=(), n=1):
            if g is None:
                a = act.do(act_(dh, src, ACT.Copy), *waits)
                d = dve.do(tt_op(dl, src, dh.bitcast(F32), ALU.subtract), a, *waits)
            else:
                a = act.do(act_(dh, src, ACT.Copy, scale=g), *waits)
                d = dve.do(stt_op(dl, src, g, dh.bitcast(F32), ALU.mult, ALU.subtract), a, *waits)
            return [a, d]

        def rstd_of(ps, dst, eps, tmp, tok, bank=None, scale=1.0):
            a = act.do(act_(tmp, ps, ACT.Sqrt, bias=eps, scale=scale), tok)
            if bank is not None:
                bank.rd.append(a)
            return dve.do(rcp_op(dst, tmp), a)

        def presum(src4, toks, acc):
            t = dve.do(tt_op(acc, src4[0], src4[1], ALU.add), toks[0], toks[1])
            t = dve.do(tt_op(acc, acc, src4[2], ALU.add), t, toks[2])
            return dve.do(tt_op(acc, acc, src4[3], ALU.add), t, toks[3])

        sqs = [t1[:, 0:2, :], t1[:, 2:4, :], t2[:, 0:2, :], t2[:, 2:4, :]]

        def add_pair(p, tok, alpha):
            b = banks[p]
            v = x[:, 2 * p:2 * p + 2, :]
            src = b.t[:, :].rearrange("p (a b) -> p a b", b=256)
            t = dve.do(stt_op(v, v, alpha, src, ALU.mult, ALU.add), tok)
            b.rd.append(t)
            return t

        def prefetch(fn):
            act.do(act_(junk, epsc[:, 0:1], fn), *me)

        def rms_parts(gname, toks, xt=None):
            fr = []
            pt, sp_t = [], []
            for p in range(4):
                a = add_pair(p, toks[p], 1.0) if xt is None else xt[p]
                pt.append(a)
                for k in (2 * p, 2 * p + 1):
                    sp_t.append(split(x[:, k, :], xh[:, k, :], xl[:, k, :], P(gname, k) if gname else None, waits=[a, fr]))
            if gname is None:
                return sp_t, None, None
            prefetch(ACT.Sqrt)
            for p in range(4):
                pt[p] = act.do(act_(sqs[p], x[:, 2 * p:2 * p + 2, :], ACT.Square), pt[p], fr)
            return sp_t, presum(sqs, pt, sqs[0]), pt

        def rms_stats(t, RT=None, nxt=None):
            acc = sqs[0]
            b = banks[7]
            pe.wait(b.take(), t)
            mm(b.t[:, 0:256], onm, acc[:, 0, :], start=True, stop=False)
            t = mm(b.t[:, 0:256], onm, acc[:, 1, :], start=False, stop=True, mark=True)
            a = act.do(act_(sqs[1][:, 0, :], b.t[:, 0:256], ACT.Sqrt, bias=epsc[:, 0:1]), t)
            r = [dve.do(rcp_op(R[:, 0, :], sqs[1][:, 0, :]), a)]
            b.rd.append(a)
            if RT is not None:
                b7 = banks[6]
                pe.wait(b7.take())
                for tt in range(2):
                    s = slice(tt * 128, tt * 128 + 128)
                    mm(b7.t[:, tt:tt + 1], acc[:, 0, s], onm[:, 0:1], start=True, stop=False)
                    t = mm(b7.t[:, tt:tt + 1], acc[:, 1, s], onm[:, 0:1], start=False, stop=True, mark=True)
                a = act.do(act_(epsc[:, 2:4], b7.t[:, 0:2], ACT.Sqrt, bias=epsc[:, 0:1]), t)
                b7.rd.append(a)
                r.append(dve.do(rcp_op(RT, epsc[:, 2:4]), a))
            if nxt is not None:
                prefetch(nxt)
            return r

        def layer_norm(gname, bname, toks, final=False, nxt=ACT.Silu):
            acc = t1[:, 0:2, :]
            yt = [add_pair(0, toks[0], ALPHA), add_pair(1, toks[1], ALPHA)]
            t = dve.do(tt_op(acc, x[:, 0:2, :], x[:, 2:4, :], ALU.add), yt[0], yt[1], *everyone())
            yt.append(add_pair(2, toks[2], ALPHA))
            t = dve.do(tt_op(acc, acc, x[:, 4:6, :], ALU.add), t, yt[2])
            yt.append(add_pair(3, toks[3], ALPHA))
            prefetch(ACT.Sqrt)
            b = banks[6]
            pe.wait(b.take(), t)
            mm(b.t[:, 0:256], onm, acc[:, 0, :], start=True, stop=False)
            mm(b.t[:, 0:256], onm, acc[:, 1, :], start=False, stop=False)
            pe.wait(yt[3])
            mm(b.t[:, 0:256], onm, x[:, 6, :], start=False, stop=False)
            m = mm(b.t[:, 0:256], onm, x[:, 7, :], start=False, stop=True, mark=True)
            mean = b.t[:, 0:256].unsqueeze(1).broadcast_to([128, 2, 256])
            b7 = banks[7]
            pe.wait(b7.take())
            qt = []
            for p in range(4):
                v = x[:, 2 * p:2 * p + 2, :]
                ct = dve.do(tt_op(v, v, mean, ALU.subtract), m, yt[p])
                qt.append(act.do(act_(sqs[p], v, ACT.Square), ct, m))
                for i in range(2):
                    t = mm(b7.t[:, 0:256], onm, sqs[p][:, i, :], start=p == 0 and i == 0, stop=p == 3 and i == 1,
                           mark=p == 3 and i == 1, waits=[qt[-1]])
            b.rd.append(ct)
            a = act.do(act_(R[:, 0, :], b7.t[:, 0:256], ACT.Sqrt, bias=epsc[:, 1:2]), t)
            b7.rd.append(a)
            r = dve.do(rcp_op(R[:, 1, :], R[:, 0, :]), a)
            prefetch(nxt)
            out_t, hi = [], []
            for k in range(9):
                if k < 8:
                    nt = dve.do(stt_op(x[:, k, :], x[:, k, :], P(gname, k), R[:, 1, :], ALU.mult, ALU.mult), r, qt[k // 2])
                    if final:
                        out_t.append([act.do(act_(x[:, k, :], x[:, k, :], ACT.Identity, bias=P(bname, k)), nt)])
                        continue
                    hi.append(act.do(act_(xh[:, k, :], x[:, k, :], ACT.Identity, bias=P(bname, k)), nt))
                if k > 0 and not final:
                    j = k - 1
                    lo = dve.do(stt_op(xl[:, j, :], x[:, j, :], P(bname, j), xh[:, j, :].bitcast(F32), ALU.add, ALU.subtract), hi[j])
                    out_t.append([hi[j], lo])
            if not final:
                for k in range(8):
                    pool.do(ts_op(x[:, k, :], x[:, k, :], P(bname, k), None, ALU.add), out_t[k])
            xready[0] = pool.last()
            return out_t

        xready = [None]
        t_lvm = []

        def ffn(wg, wu, wd, NT, xt, stats=None, half=1.0):
            Rt = None
            ht = {}
            dt_ = {}
            toks = None
            used = {}
            for j in range(NT + 2):
                if j < NT:
                    b = banks[4 + j % 4]
                    if j == 0:
                        early = gemm_fm_first([(wg, 0, b, 0), (wu, 0, b, 1), (wg, 1, banks[5], 0)], xh, xl, xt)
                        tu = early[2]
                        if stats is not None:
                            Rt = stats()
                    elif j == 1:
                        tu = gemm_fm(wu, j, b, 1, xh, xl)
                    else:
                        gemm_fm(wg, j, b, 0, xh, xl)
                        tu = gemm_fm(wu, j, b, 1, xh, xl)
                    q = j % 4
                    s, u = t1[:, q, :], t2[:, q, :]
                    hh, hl = h1[0][:, q, :], h1[1][:, q, :]
                    G, U_ = b.t[:, 0:256], b.t[:, 256:512]
                    prev = ht.get(j - 4)
                    if Rt is not None:
                        a = dve.do(tt_op(s, G, R[:, 0, :], ALU.mult), tu, Rt, prev)
                        a = act.do(act_(s, s, ACT.Silu), a)
                        a = dve.do(tt_op(s, s, R[:, 0, :], ALU.mult), a)
                        a = dve.do(tt_op(u, s, U_, ALU.mult), a)
                    else:
                        a = act.do(act_(s, G, ACT.Silu), tu, prev)
                        a = dve.do(stt_op(u, s, half, U_, ALU.mult, ALU.mult), a)
                    b.rd.append(a)
                    ht[j] = split(u, hh, hl, waits=[a, dt_.get(j - 4)])
                if j >= 2:
                    k = j - 2
                    toks = gemm_acc(wd, k, h1[0], h1[1], k % 4, k == 0, k == NT - 1, waits=ht[k])
                    dt_[k] = toks[-1]
            return toks

        def attend(nh, qf, kf, vf, bias, S, PT, st, bks, put, scale, sink=None, fr=(), slope=None, ready=(), gap=2):
            for h0 in range(0, nh, 4):
                stt = []
                for i in range(4):
                    h = h0 + i
                    b = bks[i % 2]
                    pe.wait(b.take(), *ready)
                    q, k = qf(h), kf(h)
                    mm(b.t[:, 0:128], q[:, 0:128], k[:, 0:128])
                    t = mm(b.t[:, 128:384], q[:, 128:256], k[:, 0:256], mark=True)
                    if slope is None:
                        bi = bias(h)
                        a = dve.do(stt_op(
                            S[:, i, :], b.t[:, 0:384], scale, bi, ALU.mult, ALU.add), t, *fr)
                    else:
                        a = dve.do(stt_op(
                            S[:, i, :], bias(h), slope(h), b.t[:, 0:384], ALU.mult, ALU.add), t, *fr)
                    b.rd.append(a)
                    stt.append(a)
                    if i % 2 == 1:
                        yield
                m = dve.do(red_op(st[:, 0, 0:4], S[:, :, 0:128], AX, ALU.max), *stt)
                m2 = dve.do(red_op(st[:, 0, 4:8], S[:, :, 128:384], AX, ALU.max), *stt)
                if sink is not None:
                    sk = sink(h0)
                    m = dve.do(tt_op(
                        st[:, 0, :].rearrange("p (a b) -> p a b", b=4), st[:, 0, :].rearrange("p (a b) -> p a b", b=4),
                        sk.unsqueeze(1).broadcast_to([128, 2, 4]), ALU.max), m, m2)
                m = dve.do(ts_op(st[:, 1, :], st[:, 0, :], -1.0, None, ALU.mult), m, m2)
                ex = []
                for i in range(4):
                    for sgm, sl in ((0, slice(0, 128)), (1, slice(128, 384))):
                        c = sgm * 4 + i
                        ex.append(act.do(act_(
                            S[:, i, sl], S[:, i, sl], ACT.Exp, bias=st[:, 1, c:c + 1], accum_out=st[:, 2, c:c + 1]), m))
                if sink is not None:
                    z = dve.do(tt_op(
                        st[:, 4, :].rearrange("p (a b) -> p a b", b=4), sk.unsqueeze(1).broadcast_to([128, 2, 4]),
                        st[:, 1, :].rearrange("p (a b) -> p a b", b=4), ALU.add), m)
                    z = act.do(act_(st[:, 4, :], st[:, 4, :], ACT.Exp), z)
                    z = dve.do(tt_op(st[:, 2, :], st[:, 2, :], st[:, 4, :], ALU.add), z, *ex)
                else:
                    z = ex[-1]
                for _ in range(gap):
                    yield
                r = dve.do(rcp_op(st[:, 3, :], st[:, 2, :]), z)
                n1 = dve.do(tt_op(S[:, :, 0:128], S[:, :, 0:128],
                                                      st[:, 3, 0:4].unsqueeze(2).broadcast_to([128, 4, 128]), ALU.mult), r, *ex)
                n2 = dve.do(tt_op(S[:, :, 128:384], S[:, :, 128:384],
                                                      st[:, 3, 4:8].unsqueeze(2).broadcast_to([128, 4, 256]), ALU.mult), r, *ex)
                yield
                yield
                pts = []
                for i in range(4):
                    b = bks[i % 2]
                    pe.wait(b.take(), n1, n2)
                    for j in range(3):
                        t = tr(b.t[:, j * 128:j * 128 + 128], S[:, i, j * 128:j * 128 + 128], ident, mark=j == 2)
                    a = act.do(act_(PT[:, i, :], b.t[:, 0:384], ACT.Copy), t)
                    b.rd.append(a)
                    pts.append(a)
                    if i % 2 == 1:
                        yield
                for i in range(4):
                    put(h0 + i, PT[:, i, :], vf(h0 + i), pts[i])
                    if i % 2 == 1:
                        yield

        def pv(o, pt, v, wait):
            mm(o, v[0], pt[:, 0:256], start=True, stop=False, waits=wait)
            return mm(o[:, 128:256], v[1], pt[:, 256:384], start=False, stop=True, mark=True)

        c = ins["consts"]
        ar = Arena()
        xtm = ar.get(2, 1024)
        tx = sp.dma(s_c[3], xtm, ins["x"].rearrange("(a p) d -> p a d", p=128))
        tc = sp.dma(s_c[0], cst[:, :], c[:, 0:640])
        tp = sp.dma(s_c[1], pk[:, :], ins["pack"])
        me = [dve.do(set_op(epsc[:, 0:1], 1e-6)), dve.do(set_op(epsc[:, 1:2], 1e-5)), dve.do(set_op(onm, 1.0 / 1024))]
        for q in (act, pe):
            q.wait(*me)
        for q in (act, dve, sp):
            q.wait(tp)
        xt = []
        for p in range(4):
            b = banks[p]
            pe.wait(tc, tx)
            for kk in range(2):
                for tt in range(2):
                    t = tr(b.t[:, kk * 256 + tt * 128:kk * 256 + tt * 128 + 128],
                           xtm[:, tt, (2 * p + kk) * 128:(2 * p + kk + 1) * 128], ident, mark=kk == 1 and tt == 1)
            a = dve.do(copy_op(
                x[:, 2 * p:2 * p + 2, :], b.t[:, :].rearrange("p (a b) -> p a b", b=256)), t)
            b.rd.append(a)
            xt.append(a)
        ws.prep(4)

        def even(xt):
            RT = ar.get(2)
            lat = ar.get(5, 256)
            cq, ckv = lat[:, 0:3, :], lat[:, 3:5, :]
            kpe = ar.get(2, 32)
            qkT = ar.get(32, 96)
            kvT = ar.get(2, 1024)
            uF, vT = ar.get(4, 256), ar.get(2, 512)
            gw, gwT = ar.get(4, 128), ar.get(4, 128)
            qF, kF = ar.get(8, 256), ar.get(8, 256)
            SS, sts = [ar.get(4, 384), ar.get(4, 384)], [ar.get(5, 8), ar.get(5, 8)]
            sq = ar.get(5, 256)
            rr = ar.get(64)
            cs = ar.get(2, 32)
            mk = ar.get(384)
            twk = ar.get(4, 256)
            sqt = arena[:, 0:2048]
            t_row = sp.dma(chan("s_e"), rowc[:, 0:704], ins["rowa"].partition_broadcast(128))
            t_gw = sp.dma(chan("s_e2"), gw, ins["gmw"].rearrange("g t s -> t g s"))
            t_cs = sp.dma(chan("s_e3"), cs, c[:, COFF["cosT"]:COFF["cosT"] + 64].rearrange("p (a b) -> p a b", b=32))
            t_mk = sp.dma(chan("s_e4"), mk, c[:, COFF["mask"]:COFF["mask"] + 384])
            sp_t, sqt_, _ = rms_parts("nm0", None, xt)
            ah, al = xh, xl
            toks = []
            early = gemm_fm_first([("ew_c", i, banks[i], 0) for i in range(4)], ah, al, sp_t)
            rt = rms_stats(sqt_, RT)
            for i in range(5):
                b = banks[i]
                t = early[i] if i < 4 else gemm_fm("ew_c", i, b, 0, ah, al)
                dst = cq[:, i, :] if i < 3 else ckv[:, i - 3, :]
                a = dve.do(tt_op(dst, b.t[:, 0:256], R[:, 0, :], ALU.mult), t, *rt)
                b.rd.append(a)
                q = act.do(act_(sq[:, i, :], dst, ACT.Square), a)
                toks.append([a, q])
            b = banks[5]
            t = gemm_tm("ew_pe", 0, [b], ah, al, 8, 8, 32)
            a = dve.do(tt_op(kpe, b.t[:, 0:64].rearrange("p (a b) -> p a b", b=32),
                                                 RT.unsqueeze(2).broadcast_to([128, 2, 32]), ALU.mult), t)
            b.rd.append(a)
            t_kpe = a
            sqd = []
            for i in range(5):
                dst = cq[:, i, :] if i < 3 else ckv[:, i - 3, :]
                g = P("qan", i) if i < 3 else P("kvan", i - 3)
                hh = h1[0][:, i, :] if i < 3 else h2[0][:, i - 3, :]
                hl = h1[1][:, i, :] if i < 3 else h2[1][:, i - 3, :]
                sqd.append(split(dst, hh, hl, g, waits=toks[i]))
            b = banks[6]
            pe.wait(b.take(), *[tt[1] for tt in toks])
            for kind, ks in ((0, (0, 1, 2)), (1, (3, 4))):
                for tt in range(2):
                    s = slice(tt * 128, tt * 128 + 128)
                    col = kind * 2 + tt
                    for k in ks:
                        t = mm(b.t[:, col:col + 1], sq[:, k, s], ones[:, 0:1], start=k == ks[0], stop=k == ks[-1], mark=True)
            a1 = act.do(act_(rr[:, 0:2], b.t[:, 0:2], ACT.Sqrt, bias=epsc[:, 0:1], scale=1.0 / 384), t)
            a2 = act.do(act_(rr[:, 2:4], b.t[:, 2:4], ACT.Sqrt, bias=epsc[:, 0:1], scale=1.0 / 256), t)
            b.rd += [a1, a2]
            t_rr = dve.do(rcp_op(rr[:, 4:8], rr[:, 0:4]), a1, a2)
            t_sq = t
            kv_t, q_t = {}, {}
            dve.wait(t_row, t_cs)

            def ukv(half):
                t = gemm_tm("ew_ukv", half, [banks[0], banks[1]], h2[0], h2[1], 2, 2, 512, waits=sqd[3] + sqd[4])
                for tt in range(2):
                    b = banks[tt]
                    kv_t[half, tt] = act.do(act_(
                        kvT[:, tt, half * 512:half * 512 + 512], b.t[:, :], ACT.Copy, scale=rr[:, 6 + tt:7 + tt]), t, t_rr)
                    b.rd.append(kv_t[half, tt])

            def uq(half):
                bq = [banks[2], banks[3]]
                t = gemm_tm("ew_uq", 3 * half, bq, h1[0], h1[1], 3, 1, 384, waits=sqd[0] + sqd[1] + sqd[2])
                for tt in range(2):
                    b = bq[tt]
                    i0 = half * 16 + tt * 8
                    dst = qkT[:, i0:i0 + 4, :].rearrange("p a b -> p (a b)")
                    q_t[half, tt] = act.do(act_(dst, b.t[:, 0:384], ACT.Copy, scale=rr[:, 4 + tt:5 + tt]), t, t_rr)
                    b.rd.append(q_t[half, tt])

            ot = {}
            normed = {}

            def put(h, pt, v, w):
                j = h // 2
                b = banks[6 + j % 2]
                if h % 2 == 0:
                    pe.wait(b.take())
                p0 = 64 * (h % 2)
                t = pv(b.t[p0:p0 + 64, 0:256], pt, v, [w])
                if h % 2 == 1:
                    ot[j] = split(b.t[:, 0:256], h2[0][:, j, :], h2[1][:, j, :], waits=[t])
                    b.rd += ot[j]

            def heads(half):
                s16 = slice(half * 16, half * 16 + 16)
                v = qkT[:, s16, :]
                kc_ = []
                for tt in range(2):
                    i0 = half * 16 + tt * 8 + 4
                    kk = kvT[:, tt, half * 512:half * 512 + 512].rearrange("p (h d) -> p h d", d=128)
                    kc_.append(dve.do(copy_op(qkT[:, i0:i0 + 4, 0:64], kk[:, :, 0:64]), kv_t[half, tt]))
                    kc_.append(dve.do(copy_op(
                        qkT[:, i0:i0 + 4, 64:96], kpe[:, tt, :].unsqueeze(1).broadcast_to([128, 4, 32])), t_kpe))
                sv = sqt[:, 0:1536].rearrange("p (a b) -> p a b", b=96)
                a = act.do(act_(sv, v, ACT.Square), *kc_, q_t[half, 0], q_t[half, 1], normed.get(("sum", half - 1)))
                yield
                rs = rr[:, 8 + half * 16:24 + half * 16]
                a = dve.do(red_op(rs, sv, AX, ALU.add), a)
                normed["sum", half] = a
                rq = sqt[:, 1536 + half * 16:1552 + half * 16]
                a = act.do(act_(rq, rs, ACT.Sqrt, bias=epsc[:, 0:1], scale=1.0 / 96), a)
                a = dve.do(rcp_op(rs, rq), a)
                yield
                a = dve.do(tt_op(v, v, rs.unsqueeze(2).broadcast_to([128, 16, 96]), ALU.mult), a)
                gm = []
                for w in range(2):
                    g = rowc[:, w * 96:w * 96 + 96].unsqueeze(1).broadcast_to([128, 4, 96])
                    for tt in range(2):
                        i0 = half * 16 + tt * 8 + w * 4
                        gm.append(dve.do(tt_op(qkT[:, i0:i0 + 4, :], qkT[:, i0:i0 + 4, :], g, ALU.mult), a))
                yield
                x1 = v[:, :, 64:80].rearrange("p (t h) d -> p t h d", t=2)
                x2 = v[:, :, 80:96].rearrange("p (t h) d -> p t h d", t=2)
                C = cs[:, 0, :].rearrange("p (t d) -> p t d", t=2).unsqueeze(2).broadcast_to([128, 2, 8, 16])
                Sn = cs[:, 1, :].rearrange("p (t d) -> p t d", t=2).unsqueeze(2).broadcast_to([128, 2, 8, 16])
                tm_ = [twk[:, i, 0:256].rearrange("p (t h d) -> p t h d", t=2, h=8) for i in range(4)]
                m1 = dve.do(tt_op(tm_[0], x1, C, ALU.mult), *gm, *normed.get(("rot", half - 1), []))
                m2 = dve.do(tt_op(tm_[1], x2, Sn, ALU.mult))
                m3 = dve.do(tt_op(tm_[2], x2, C, ALU.mult))
                m4 = dve.do(tt_op(tm_[3], x1, Sn, ALU.mult))
                r1 = dve.do(tt_op(x1, tm_[0], tm_[1], ALU.subtract), m1, m2, m3, m4)
                r2 = dve.do(tt_op(x2, tm_[2], tm_[3], ALU.add), m3, m4)
                normed["rot", half] = [r1, r2]
                yield
                tf = []
                for w, dst in ((0, qF), (1, kF)):
                    for h2_ in range(0, 4, 2):
                        b = banks[4 + w * 2 + h2_ // 2]
                        pe.wait(b.take(), r1, r2)
                        for hh in range(2):
                            for tt in range(2):
                                t = tr(b.t[0:96, hh * 256 + tt * 128:hh * 256 + tt * 128 + 128],
                                       qkT[:, half * 16 + tt * 8 + w * 4 + h2_ + hh, :], ident, mark=hh == 1 and tt == 1)
                        h0 = half * 4 + h2_
                        a = act.do(act_(
                            dst[0:96, h0:h0 + 2, :], b.t[0:96, :].rearrange("p (a b) -> p a b", b=256), ACT.Copy), t)
                        b.rd.append(a)
                        tf.append(a)
                yield
                o = half * 4
                yield from attend(4, lambda h: qF[0:96, o + h, :], lambda h: kF[0:96, o + h, :],
                                  lambda h: [kvT[:, n, (o + h) * 128 + 64:(o + h) * 128 + 128] for n in range(2)],
                                  lambda h: mk, SS[half], SS[half], sts[half], [banks[4], banks[5]],
                                  lambda h, *r: put(o + h, *r), float(96 ** -0.5), ready=tf)

            ukv(0)
            uq(0)
            side.append(heads(0))
            dve.wait(t_mk)
            ukv(1)
            step()
            uq(1)
            step()
            side.append(heads(1))
            t = gemm_tm("ew_v", 0, [banks[2], banks[3]], ah, al, 8, 2, 512, after=step)
            vt = []
            for tt in range(2):
                b = banks[2 + tt]
                vt.append(act.do(act_(vT[:, tt, :], b.t[:, :], ACT.Gelu_apprx_tanh,
                                                                  scale=RT[:, tt:tt + 1]), t, *rt))
                b.rd.append(vt[-1])
            v8 = vT.rearrange("p t (g d) -> p (t g) d", d=128)
            s8 = sq[:, 0:4, :].rearrange("p a b -> p (a b)").rearrange("p (a b) -> p a b", b=128)
            vn = act.do(act_(s8, v8, ACT.Square), *vt, t_sq)
            ugs = []
            for i in range(4):
                b = banks[i % 2]
                t = gemm_fm("ew_u", i, b, 0, ah, al)
                a = dve.do(tt_op(uF[:, i, :], b.t[:, 0:256], R[:, 0, :], ALU.mult), t)
                b.rd.append(a)
                ugs.append(act.do(act_(uF[:, i, :], uF[:, i, :], ACT.Gelu_apprx_tanh), a))
                if i == 0:
                    vn = dve.do(red_op(rr[:, 40:48], s8, AX, ALU.add), vn)
                    vn = act.do(act_(rr[:, 48:56], rr[:, 40:48], ACT.Sqrt, bias=epsc[:, 0:1], scale=1.0 / 128), vn)
                if i == 1:
                    vn = dve.do(rcp_op(rr[:, 40:48], rr[:, 48:56]), vn)
                    t_v = dve.do(tt_op(v8, v8, rr[:, 40:48].unsqueeze(2).broadcast_to([128, 8, 128]), ALU.mult), vn)
                    b = banks[2]
                    pe.wait(b.take(), t_gw)
                    for g in range(4):
                        t = tr(b.t[:, g * 128:g * 128 + 128], gw[:, g, :], ident, mark=g == 3)
                    a = act.do(act_(gwT, b.t[:, :].rearrange("p (a b) -> p a b", b=128), ACT.Copy), t)
                    b.rd.append(a)
                    t_gw = dve.do(set_op(gwT[64:128, :, 0:64], 0.0), a)
                step()
            at_t = []
            for g in range(4):
                b = banks[g]
                pe.wait(b.take(), t_v, t_gw)
                for n in range(2):
                    t = mm(b.t[:, n * 128:n * 128 + 128], vT[:, n, g * 128:g * 128 + 128], gwT[:, g, :],
                           mark=n == 1)
                tw = lat[:, g, :]
                bB = rowc[:, 192 + g * 128:192 + g * 128 + 128].unsqueeze(1).broadcast_to([128, 2, 128])
                a = dve.do(stt_op(
                    tw.rearrange("p (a b) -> p a b", b=128), b.t[:, 0:256].rearrange("p (a b) -> p a b", b=128),
                    P("gmv", g), bB, ALU.mult, ALU.add), t, *sqd[g])
                b.rd.append(a)
                a = dve.do(tt_op(tw, tw, uF[:, g, :], ALU.mult), a, ugs[g])
                at_t.append(split(tw, h1[0][:, g, :], h1[1][:, g, :], waits=[a, t]))
            step()
            for k in range(4):
                gemm_acc("ew_out", k, h1[0], h1[1], k, k == 0, False, waits=at_t[k])
                step()
            for k in range(4):
                while k not in ot:
                    step()
                toks = gemm_acc("ew_out", 4 + k, h2[0], h2[1], k, False, k == 3, waits=ot[k])
                step()
            finish()
            return toks

        def odd(xt):
            ar = Arena()
            fr = everyone()
            RT = ar.get(2)
            qF, kF = ar.get(8, 256), ar.get(8, 256)
            vT = ar.get(2, 2048)
            sg = ar.get(16, 256)
            cc, ss = ar.get(2, 256), ar.get(2, 256)
            dtr = ar.get(4, 256)
            AT = ar.get(2, 384)
            o = ar.get(4, 256)
            osq = ar.get(4, 256)
            tq = ar.get(2, 512)
            Ro = ar.get(2, 256)
            s_o = [chan(f"s_o{i}") for i in range(3)]
            tb = [sp.dma(s_o[0], cc, c[:, COFF["cc"]:COFF["cc"] + 512].rearrange("p (a b) -> p a b", b=256), fr),
                  sp.dma(s_o[1], ss, c[:, COFF["ss"]:COFF["ss"] + 512].rearrange("p (a b) -> p a b", b=256), fr),
                  sp.dma(s_o[2], dtr, c[:, COFF["dtr"]:COFF["dtr"] + 1024].rearrange("p (a b) -> p a b", b=256), fr)]
            dve.wait(*fr)
            act.wait(*fr)
            sp_t, sqt_, _ = rms_parts("nm1", xt)
            rt = ()
            vt = []
            for cg in range(4):
                bq = [banks[0], banks[1]] if cg % 2 == 0 else [banks[2], banks[3]]
                t = gemm_tm("ow_v", cg * 4, bq, xh, xl, 8, 2, 512, wk=sp_t)
                if cg == 0:
                    rt = rms_stats(sqt_, RT)
                for tt in range(2):
                    b = bq[tt]
                    a = act.do(act_(
                        vT[:, tt, cg * 512:cg * 512 + 512], b.t[:, :], ACT.Copy, scale=RT[:, tt:tt + 1]), t, *rt)
                    b.rd.append(a)
                    vt.append(a)
            dve.wait(*tb)
            qt = {}
            prev = None
            for i in range(8):
                h, w = i // 2, i % 2
                b = banks[4 + i % 2]
                gemm_fm("ow_qk", 2 * i, b, 0, xh, xl)
                t = gemm_fm("ow_qk", 2 * i + 1, b, 1, xh, xl)
                tt_ = tq[:, 0, :].rearrange("p (a b) -> p a b", b=256)
                ts_ = tq[:, 1, :].rearrange("p (a b) -> p a b", b=256)
                a = dve.do(tt_op(
                    tt_, b.t[:, :].rearrange("p (a b) -> p a b", b=256), R[:, 0:1, :].broadcast_to([128, 2, 256]), ALU.mult), t, prev, *rt)
                b.rd.append(a)
                s0 = dve.do(tt_op(ts_[:, 0, :], tt_[:, 1, :], ss[:, 0, :], ALU.mult), a)
                s1 = dve.do(tt_op(ts_[:, 1, :], tt_[:, 0, :], ss[:, 1, :], ALU.mult), a)
                a = dve.do(tt_op(tt_, tt_, cc, ALU.mult), s0, s1)
                dst = (qF if w == 0 else kF)[:, 2 * h:2 * h + 2, :]
                prev = dve.do(tt_op(dst, tt_, ts_, ALU.add), a)
                qt[h, w] = prev
            gt = {}
            ot = {}
            hb = [h1, h2]
            ows = {}

            def head(h):
                b = banks[5]
                pe.wait(b.take(), qt[h, 0], qt[h, 1])
                for d in range(2):
                    mm(b.t[:, 0:256], kF[:, 2 * h + d, 0:128], qF[:, 2 * h + d, :], start=d == 0, stop=d == 1)
                for d in range(2):
                    t = mm(b.t[:, 256:384], kF[:, 2 * h + d, 128:256], qF[:, 2 * h + d, 128:256], start=d == 0, stop=d == 1, mark=True)
                a = dve.do(stt_op(
                    AT[:, h % 2, 0:256], b.t[:, 0:256], 0.0625, dtr[:, h, :], ALU.mult, ALU.mult), t, ot.get((h - 2, "pe")))
                a2 = dve.do(stt_op(
                    AT[:, h % 2, 256:384], b.t[:, 256:384], 0.0625, dtr[:, h, 0:128], ALU.mult, ALU.mult), t)
                b.rd.append(a2)
                yield
                ev = []
                for pr in range(2):
                    b = banks[6 + pr]
                    pe.wait(b.take(), a, a2, *vt)
                    for e_ in range(2):
                        ec = h * 512 + (pr * 2 + e_) * 128
                        ob = b.t[:, e_ * 256:e_ * 256 + 256]
                        mm(ob, vT[:, 0, ec:ec + 128], AT[:, h % 2, 0:256], start=e_ == 0, stop=False)
                        t = mm(ob[:, 128:256], vT[:, 1, ec:ec + 128], AT[:, h % 2, 256:384], start=False, stop=True, mark=True)
                    src = b.t[:, :].rearrange("p (a b) -> p a b", b=256)
                    a1 = act.do(act_(o[:, 2 * pr:2 * pr + 2, :], src, ACT.Copy), t, ot.get((h - 1, "dve")))
                    b.rd.append(a1)
                    sq_ = act.do(act_(osq[:, 2 * pr:2 * pr + 2, :], o[:, 2 * pr:2 * pr + 2, :], ACT.Square), a1, ot.get((h - 1, "sum")))
                    ev.append(sq_)
                ot[h, "pe"] = t
                yield
                a = dve.do(tt_op(osq[:, 0:2, :], osq[:, 0:2, :], osq[:, 2:4, :], ALU.add), *ev)
                b = banks[5]
                pe.wait(b.take(), a)
                mm(b.t[:, 0:256], ones, osq[:, 0, :], start=True, stop=False)
                t = mm(b.t[:, 0:256], ones, osq[:, 1, :], start=False, stop=True, mark=True)
                ot[h, "sum"] = t
                r = rstd_of(b.t[:, 0:256], Ro[:, 1, :], epsc[:, 0:1], Ro[:, 0, :], [t, ot.get((h - 1, "dve"))], bank=b, scale=1.0 / 512)
                yield
                dst = hb[h % 2]
                res = []
                for e_ in range(4):
                    i = h * 4 + e_
                    a = dve.do(stt_op(
                        o[:, e_, :], o[:, e_, :], P("ron", i), Ro[:, 1, :], ALU.mult, ALU.mult), r)
                    a = dve.do(tt_op(o[:, e_, :], o[:, e_, :], sg[:, i, :], ALU.mult), a, gt[i])
                    res.append(split(o[:, e_, :], dst[0][:, e_, :], dst[1][:, e_, :], waits=[a, ows.get(h - 2)]))
                    if e_ == 1:
                        yield
                ot[h, "dve"] = [res[-1][0], res[-1][1]]
                ot[h] = res

            for i in range(16):
                b = banks[i % 4]
                t = gemm_fm("ow_g", i, b, 0, xh, xl)
                a = dve.do(tt_op(sg[:, i, :], b.t[:, 0:256], R[:, 0, :], ALU.mult), t)
                b.rd.append(a)
                gt[i] = act.do(act_(sg[:, i, :], sg[:, i, :], ACT.Silu), a)
                if i in (6, 12):
                    side.append(head(0 if i == 6 else 1))
                step()
            finish()
            for h in range(4):
                if h < 3 and (h + 1) not in ot:
                    side.append(head(h + 1))
                for k in range(4):
                    if k == 0 and h not in ot:
                        finish()
                    toks = gemm_acc("ow_out", h * 4 + k, hb[h % 2][0], hb[h % 2][1], k, h == 0 and k == 0, h == 3 and k == 3,
                                    waits=ot[h][k])
                    ows[h] = toks[-1]
                    step()
                finish()
            return toks

        def hybrid(l, xt):
            ar = Arena()
            fr = everyone()
            for q in (dve, act, pool):
                q.wait(*fr)
            qb, kb, vb = ar.get(4, 256), ar.get(4, 256), ar.get(2, 512)
            qc, kc, vc = ar.get(4, 256), ar.get(1, 256), ar.get(2, 128)
            S = ar.get(4, 384)
            PT = S
            bb = ar.get(4, 384)
            pre = ar.get(4, 256)
            cv = ar.get(12, 256)
            kv0 = ar.at
            kT, vT = ar.get(8, 128), ar.get(8, 128)
            negd = ar.get(384)
            st = ar.get(5, 8)
            sm = ar.get(24, 8)
            nr = ar.get(2, 16)
            zf = ar.get(4, 256)
            DT, nLT, AT, kbg, T, TT = (ar.get(8, 128) for _ in range(6))
            Y, U_, wT, S1 = DT, vT, nLT[:, 0:4, :], nLT[:, 4:8, :]
            mgs = [t1[:, 0:2, :], t1[:, 2:4, :], t2[:, 0:2, :], t2[:, 2:4, :]]
            chs = [chan(f"s_m{l}{i}") for i in range(3)]
            tb = [sp.dma(chs[0], rowc[:, 0:ROWC], ins[f"rowc{l}"].partition_broadcast(128), fr),
                  sp.dma(chs[1], bb, ins[f"relb{l}"], fr),
                  sp.dma(chs[2], negd, c[:, COFF["negd"]:COFF["negd"] + 384], fr)]
            if l == 0:
                lvf = arena[:, kv0:kv0 + 1792].rearrange("p (a b) -> p a b", b=128)
                t_lvm.append(sp.dma(s_c[2], lvf, ins["lvmask"], fr))
            ROW = {"vb": (0, 512), "vc": (512, 128), "ba": (640, 8), "al": (648, 4), "dt": (652, 4), "sk": (656, 8)}

            def row(n):
                return rowc[:, ROW[n][0]:ROW[n][0] + ROW[n][1]]

            qbt = []
            early = gemm_fm_first([(f"mw_qkb{l}", i, banks[i], 0) for i in range(3)], xh, xl, xt)
            for i in range(8):
                b = banks[i % 4]
                t = early[i] if i < 3 else gemm_fm(f"mw_qkb{l}", i, b, 0, xh, xl)
                dst, nm = (qb[:, i, :], "bqb") if i < 4 else (kb[:, i - 4, :], "bkb")
                a = act.do(act_(dst, b.t[:, 0:256], ACT.Identity, bias=P(f"{nm}{l}", i % 4)), t)
                b.rd.append(a)
                qbt.append(a)
            t = gemm_tm(f"mw_vb{l}", 0, [banks[2], banks[3]], xh, xl, 8, 2, 512)
            dve.wait(*tb)
            for tt in range(2):
                b = banks[2 + tt]
                a = dve.do(tt_op(vb[:, tt, :], b.t[:, :], row("vb"), ALU.add), t)
                b.rd.append(a)
                qbt.append(a)
            oB, oBt, oC, oCt = h1, {}, h2, {}

            def putB(h, pt, v, w):
                b = banks[2 + h % 2]
                pe.wait(b.take())
                t = pv(b.t[:, 0:256], pt, v, [w])
                oBt[h] = split(b.t[:, 0:256], oB[0][:, h, :], oB[1][:, h, :], waits=[t])
                b.rd += oBt[h]

            def putC(h, pt, v, w):
                j, g = h // 2, h % 2
                b = banks[2 + j % 2]
                if g == 0:
                    pe.wait(b.take())
                t = pv(b.t[64 * g:64 * g + 64, 0:256], pt, v, [w])
                if g == 1:
                    oCt[j] = split(b.t[:, 0:256], oC[0][:, j, :], oC[1][:, j, :], waits=[t])
                    b.rd += oCt[j]

            done = {}

            def both():
                yield from attend(4, lambda h: qb[:, h, :], lambda h: kb[:, h, :],
                                  lambda h: [vb[:, n, h * 128:h * 128 + 128] for n in range(2)],
                                  lambda h: bb[:, h, :], S, PT, st, [banks[2], banks[3]], putB, float(128 ** -0.5), ready=qbt)
                done["B"] = 1
                while "c" not in done:
                    yield

                def slope(h):
                    hh = (h % 2) * 4 + h // 2
                    return float(2.0 ** -(hh + 1))

                yield from attend(8, lambda h: qc[64 * (h % 2):64 * (h % 2) + 64, h // 2, :],
                                  lambda h: kc[64 * (h % 2):64 * (h % 2) + 64, 0, :],
                                  lambda h: [vc[:, n, 64 * (h % 2):64 * (h % 2) + 64] for n in range(2)],
                                  lambda h: negd, S, PT, st, [banks[2], banks[3]], putC, 1.0,
                                  sink=lambda h0: row("sk")[:, h0:h0 + 4], slope=slope, ready=done["c"])
                done["attn"] = everyone()

            side.append(both())
            if l == 0:
                t_lvm.append(dve.do(copy_op(lvm[:, :, :], lvf), *t_lvm))
            ct = []
            for i in range(5):
                b = banks[i % 2]
                t = gemm_fm(f"mw_c{l}", i, b, 0, xh, xl)
                if i < 4:
                    a = dve.do(ts_op(qc[:, i, :], b.t[:, 0:256], P(f"bqc{l}", i), 0.125, ALU.add, ALU.mult), t)
                else:
                    a = dve.do(ts_op(kc[:, 0, :], b.t[:, 0:256], P(f"bkc{l}", 0), None, ALU.add), t)
                b.rd.append(a)
                ct.append(a)
                step()
            b = banks[2]
            t = gemm_tm(f"mw_c{l}", 5, [b], xh, xl, 8, 8, 128)
            a = dve.do(tt_op(vc, b.t[:, 0:256].rearrange("p (a b) -> p a b", b=128),
                                                 row("vc").unsqueeze(1).broadcast_to([128, 2, 128]), ALU.add), t)
            b.rd.append(a)
            ct.append(a)
            done["c"] = ct
            step()
            b = banks[3]
            t = gemm_tm(f"mw_ba{l}", 0, [b], xh, xl, 8, 8, 8)
            BA, BE, G, GC, KD, EG, W0, W1, W2, W3, EA, BG = (sm[:, 2 * i:2 * i + 2, :] for i in range(12))
            a = dve.do(tt_op(BA, b.t[:, 0:16].rearrange("p (a b) -> p a b", b=8),
                                                 row("ba").unsqueeze(1).broadcast_to([128, 2, 8]), ALU.add), t)
            b.rd.append(a)

            def f8(v):
                return v[:, 0, :]

            def f24(v):
                return v[:, 0, :].rearrange("p (n h) -> p n h", h=4)

            def small(t):
                dv = dve.do
                be = act.do(act_(f24(BE), BA[:, :, 0:4], ACT.Sigmoid), t)
                a = dv(tt_op(f24(W0), BA[:, :, 4:8], row("dt").unsqueeze(1).broadcast_to([128, 2, 4]), ALU.add), t)
                ea = act.do(act_(EA[:, 0, 0:4], row("al"), ACT.Exp), a, *tb)
                n = dv(ts_op(f8(W1), f8(W0), -1.0, None, ALU.mult), a)
                n = dv(tt_op(f8(W1), f8(W1), f8(W0), ALU.min), n)
                y = act.do(act_(f8(W1), f8(W1), ACT.Exp), n)
                yield
                s = dv(ts_op(f8(W2), f8(W1), 2.0, None, ALU.add), y)
                s = dv(rcp_op(f8(W3), f8(W2)), s)
                s = dv(tt_op(f8(W1), f8(W1), f8(W3), ALU.mult), s)
                s = dv(tt_op(f8(W2), f8(W1), f8(W1), ALU.mult), s)
                s = dv(ts_op(f8(W3), f8(W2), 2.0 / 17, 2.0 / 15, ALU.mult, ALU.add), s)
                for cf in (13, 11, 9, 7, 5, 3, 1):
                    s = dv(tt_op(f8(W3), f8(W3), f8(W2), ALU.mult), s)
                    s = dv(ts_op(f8(W3), f8(W3), 2.0 / cf, None, ALU.add), s)
                    if cf in (9, 3):
                        yield
                s = dv(tt_op(f8(W3), f8(W3), f8(W1), ALU.mult), s)
                yield
                s = dv(stt_op(f8(W3), f8(W0), 0.0, f8(W3), ALU.max, ALU.add), s)
                s = dv(stt_op(f24(G), f24(W3), -1.0, EA[:, 0:1, 0:4].broadcast_to([128, 2, 4]),
                                                        ALU.mult, ALU.mult), s, ea)
                yield
                b = banks[3]
                pe.wait(b.take(), s, tc)
                mm(b.t[:, 0:8], Ucum, f8(G))
                t = mm(b.t[:, 8:16], ones, f8(G), mark=True)
                a = dv(copy_op(f8(GC), b.t[:, 0:8]), t)
                k = dv(tt_op(f8(KD), b.t[:, 8:16], f8(GC), ALU.subtract), a)
                b.rd.append(k)
                k = act.do(act_(f8(KD), f8(KD), ACT.Exp), k)
                g = act.do(act_(f8(EG), f8(GC), ACT.Exp), a)
                done["sm"] = [dv(tt_op(f8(BG), f8(EG), f8(BE), ALU.mult), g, be), k]

            side.append(small(a))
            cvt, ready, prt = {}, {}, {}

            def conv(i):
                y, pr = cv[:, i, :], pre[:, i % 4, :]
                a = ready[i]
                for d in (2, 3):
                    a = dve.do(stt_op(
                        y[:, d:256], pr[:, 0:256 - d], P(f"cw{l}", (3 - d) * 12 + i), y[:, d:256], ALU.mult, ALU.add), a)
                prt[i] = a
                if i % 2 == 1:
                    v = cv[:, i - 1:i + 1, :]
                    cvt[i - 1] = cvt[i] = act.do(act_(v, v, ACT.Silu), prt[i - 1], a)

            for i in range(12):
                b = banks[i % 2]
                t = gemm_fm(f"mw_a{l}", i, b, 0, xh, xl)
                pr = pre[:, i % 4, :]
                y = cv[:, i, :]
                a = act.do(act_(pr, b.t[:, 0:256], ACT.Identity, bias=P(f"bqa{l}", i)), t, prt.get(i - 4))
                b.rd.append(a)
                a2 = act.do(act_(y, pr, ACT.Copy, scale=P(f"cw{l}", 36 + i)), a)
                a = pool.do(ts_op(R[:, i % 2, :], pr, P(f"cw{l}", 24 + i), None, ALU.mult), a)
                ready[i] = pool.do(tt_op(y[:, 1:256], y[:, 1:256], R[:, i % 2, 0:255], ALU.add), a, a2)
                if i:
                    conv(i - 1)
                step()
            conv(11)
            oAt, zt = {}, []

            def inv_diag(rows, n, sqs_of, eps, scale, D, tok):
                b = banks[4]
                pe.wait(b.take(), *tok)
                for i in range(n):
                    t = mm(b.t[:, i:i + 1], sqs_of(i), ones[:, 0:1], mark=i == n - 1)
                a = act.do(act_(rows[:, 0, 0:n], b.t[:, 0:n], ACT.Sqrt, bias=eps, scale=scale), t)
                b.rd.append(a)
                a = dve.do(rcp_op(rows[:, 1, 0:n], rows[:, 0, 0:n]), a)
                dt = []
                for i in range(0, n, 4):
                    dt.append(dve.do(tt_op(D(i), ident.unsqueeze(1).broadcast_to([128, 4, 128]),
                                           rows[:, 1, i:i + 4].unsqueeze(2).broadcast_to([128, 4, 128]), ALU.mult), a))
                return dt

            def delta():
                bk = banks[4:8]
                sqp = [pre[:, 0:2, :], pre[:, 2:4, :]] + [
                    DT[:, 4 * i:4 * i + 4, :].rearrange("p (a b) c -> p a (b c)", b=2) for i in range(2)]
                qt_ = []
                for p in range(4):
                    qt_.append(act.do(act_(sqp[p], cv[:, 2 * p:2 * p + 2, :], ACT.Square), cvt[2 * p], cvt[2 * p + 1], cvt[11]))
                yield

                def dia(i):
                    return (T if i < 8 else TT)[:, i % 8:i % 8 + 4, :]

                dt = inv_diag(nr, 16, lambda i: sqp[i // 4][:, i // 2 % 2, (i % 2) * 128:(i % 2) * 128 + 128],
                              epsc[:, 0:1], 1.0, dia, qt_)
                yield
                nt = []
                for p in range(4):
                    v = cv[:, 2 * p:2 * p + 2, :]
                    b = bk[p]
                    pe.wait(b.take(), dt[p])
                    t = mm(b.t[:, :], ones, dia(4 * p).rearrange("p a b -> p (a b)"), mark=True)
                    src = b.t[:, :].rearrange("p (a b) -> p a b", b=256)
                    scl = float(128 ** -0.5) if p < 2 else 1.0
                    nt.append(dve.do(stt_op(v, v, scl, src, ALU.mult, ALU.mult), t))
                    b.rd.append(nt[-1])
                yield
                while "sm" not in done:
                    yield
                smt = done["sm"]
                q_, k_, v_ = cv[:, 0:4, :], cv[:, 4:8, :], cv[:, 8:12, :]
                DG = T
                idb = ident.unsqueeze(1).broadcast_to([128, 4, 128])
                dg = []
                for n in range(2):
                    s4 = slice(4 * n, 4 * n + 4)
                    dg.append([dve.do(tt_op(
                        DG[:, s4, :], idb, f8(GC)[:, s4].unsqueeze(2).broadcast_to([128, 4, 128]), ALU.mult), t, *smt),
                        dve.do(tt_op(
                            TT[:, s4, :], idb, f8(BE)[:, s4].unsqueeze(2).broadcast_to([128, 4, 128]), ALU.mult), t, *smt)])
                kt, vt_, kg = [], [], []
                for n in range(2):
                    b, b2 = bk[2 * n], bk[2 * n + 1]
                    s4 = slice(4 * n, 4 * n + 4)
                    pe.wait(b.take(), *nt)
                    for h in range(4):
                        t = tr(b.t[:, h * 128:h * 128 + 128], k_[:, h, n * 128:n * 128 + 128], ident, mark=h == 3)
                    src = b.t[:, :].rearrange("p (a b) -> p a b", b=128)
                    a = act.do(act_(kT[:, s4, :], src, ACT.Copy), t, *t_lvm)
                    b.rd.append(a)
                    pe.wait(b2.take(), *[cvt[8 + h] for h in range(4)])
                    for h in range(4):
                        t = tr(b2.t[:, h * 128:h * 128 + 128], v_[:, h, n * 128:n * 128 + 128], ident, mark=h == 3)
                    src = b2.t[:, :].rearrange("p (a b) -> p a b", b=128)
                    be = f8(BE)[:, s4].unsqueeze(2).broadcast_to([128, 4, 128])
                    v = dve.do(tt_op(vT[:, s4, :], src, be, ALU.mult), t, *smt)
                    b2.rd.append(v)
                    vt_.append(v)
                    bg = f8(BG)[:, s4].unsqueeze(2).broadcast_to([128, 4, 128])
                    kg.append(dve.do(tt_op(kbg[:, s4, :], kT[:, s4, :], bg, ALU.mult), a))
                    if n == 0:
                        kd = f8(KD)[:, s4].unsqueeze(2).broadcast_to([128, 4, 128])
                        kg.append(dve.do(tt_op(kT[:, s4, :], kT[:, s4, :], kd, ALU.mult), kg[-1]))
                    yield
                ws_ = []
                for n in range(2):
                    s4 = slice(4 * n, 4 * n + 4)
                    b, b2 = bk[2 * n], bk[2 * n + 1]
                    pe.wait(b.take(), b2.take(), *dg[n])
                    t = mm(b.t[:, :], ones, DG[:, s4, :].rearrange("p a b -> p (a b)"), mark=True)
                    t2_ = mm(b2.t[:, :], ones, TT[:, s4, :].rearrange("p a b -> p (a b)"), mark=True)
                    ds = []
                    for h in range(4):
                        s = 4 * n + h
                        ds.append(dve.do(stt_op(
                            DT[:, s, :], b.t[:, h * 128:h * 128 + 128], f8(GC)[:, s:s + 1], NEGU, ALU.subtract, ALU.add), t))
                    if n == 1:
                        src = b.t[:, :].rearrange("p (a b) -> p a b", b=128)
                        qe = act.do(act_(pre.rearrange("p a (b c) -> p (a b) c", c=128)[:, 0:4, :], src, ACT.Exp), ds[-1], *nt)
                        b.rd.append(qe)
                    b.rd.append(ds[-1])
                    dte = act.do(act_(DT[:, s4, :], DT[:, s4, :], ACT.Exp), *ds)
                    src2 = b2.t[:, :].rearrange("p (a b) -> p a b", b=128)
                    w = dve.do(tt_op(nLT[:, s4, :], DT[:, s4, :], src2, ALU.mult), dte, t2_)
                    b2.rd.append(w)
                    ws_.append(dve.do(tt_op(nLT[:, s4, :], nLT[:, s4, :],
                                            nSU.unsqueeze(1).broadcast_to([128, 4, 128]), ALU.mult), w))
                    yield
                ids = [[pool.do(copy_op(v[:, 4 * n:4 * n + 4, :], idb), t2_) for v in (T, TT)] for n in range(2)]
                for n in range(2):
                    s4 = slice(4 * n, 4 * n + 4)
                    b, b2 = bk[2 * n], bk[2 * n + 1]
                    pe.wait(b.take(), b2.take())
                    for h in range(4):
                        ks = k_[:, h, n * 128:n * 128 + 128]
                        mm(b.t[:, h * 128:h * 128 + 128], ks, ks)
                    for h in range(4):
                        ks = k_[:, h, n * 128:n * 128 + 128]
                        t = mm(b2.t[:, h * 128:h * 128 + 128], ks, q_[:, h, n * 128:n * 128 + 128], mark=True)
                    src = b.t[:, :].rearrange("p (a b) -> p a b", b=128)
                    src2 = b2.t[:, :].rearrange("p (a b) -> p a b", b=128)
                    l_ = dve.do(tt_op(nLT[:, s4, :], nLT[:, s4, :], src, ALU.mult), t, ws_[n])
                    b.rd.append(l_)
                    at = dve.do(tt_op(AT[:, s4, :], DT[:, s4, :], src2, ALU.mult), t)
                    b2.rd.append(at)
                    done["L", n] = l_
                    done["AT", n] = at
                yield
                qd = dve.do(tt_op(pre.rearrange("p a (b c) -> p (a b) c", c=128)[:, 0:4, :],
                                                      pre.rearrange("p a (b c) -> p (a b) c", c=128)[:, 0:4, :],
                                                      q_[:, :, 128:256], ALU.mult), qe, *nt)
                tt, ttt = {}, {}
                for n in range(2):
                    s4 = slice(4 * n, 4 * n + 4)
                    b = bk[n]
                    pe.wait(b.take(), done["L", n])
                    for h in range(4):
                        t = tr(b.t[:, h * 128:h * 128 + 128], nLT[:, 4 * n + h, :], ident, mark=h == 3)
                    src = b.t[:, :].rearrange("p (a b) -> p a b", b=128)
                    tt[n] = dve.do(pred_op(
                        T[:, s4, :], lvm[:, 0:1, :].broadcast_to([128, 4, 128]), src), t, ids[n][0], *t_lvm)
                    b.rd.append(tt[n])
                    ttt[n] = dve.do(pred_op(
                        TT[:, s4, :], lvm[:, 7:8, :].broadcast_to([128, 4, 128]), nLT[:, s4, :]), ids[n][1], tt[n])
                yield
                for lv in range(1, 7):
                    yt_ = {}
                    for n in range(2):
                        s4 = slice(4 * n, 4 * n + 4)
                        b = bk[n]
                        pe.wait(b.take(), tt[n], ttt[n])
                        for h in range(4):
                            s = 4 * n + h
                            t = mm(b.t[:, h * 128:h * 128 + 128], nLT[:, s, :], T[:, s, :], mark=h == 3)
                        src = b.t[:, :].rearrange("p (a b) -> p a b", b=128)
                        yt_[n] = act.do(act_(Y[:, s4, :], src, ACT.Copy), t)
                        b.rd.append(yt_[n])
                    yield
                    for n in range(2):
                        s4 = slice(4 * n, 4 * n + 4)
                        b, b2 = (bk[2], bk[3]) if n == 0 else (bk[0], bk[1])
                        pe.wait(yt_[n])
                        if lv < 6:
                            pe.wait(b.take())
                            for h in range(4):
                                s = 4 * n + h
                                t = mm(b.t[:, h * 128:h * 128 + 128], TT[:, s, :], Y[:, s, :], mark=h == 3)
                        pe.wait(b2.take())
                        for h in range(4):
                            s = 4 * n + h
                            t2_ = mm(b2.t[:, h * 128:h * 128 + 128], Y[:, s, :], TT[:, s, :], mark=h == 3)
                        if lv < 6:
                            src = b.t[:, :].rearrange("p (a b) -> p a b", b=128)
                            tt[n] = dve.do(pred_op(
                                T[:, s4, :], lvm[:, lv:lv + 1, :].broadcast_to([128, 4, 128]), src), t2_)
                            b.rd.append(tt[n])
                        src2 = b2.t[:, :].rearrange("p (a b) -> p a b", b=128)
                        ttt[n] = dve.do(pred_op(
                            TT[:, s4, :], lvm[:, 7 + lv:8 + lv, :].broadcast_to([128, 4, 128]), src2), t2_)
                        b2.rd.append(ttt[n])
                    yield
                ut = []
                for n in range(2):
                    b = bk[n]
                    pe.wait(b.take(), ttt[n], *vt_, *kg)
                    for h in range(4):
                        s = 4 * n + h
                        t = mm(b.t[:, h * 128:h * 128 + 128], TT[:, s, :], vT[:, s, :], mark=h == 3)
                    src = b.t[:, :].rearrange("p (a b) -> p a b", b=128)
                    ut.append(act.do(act_(U_[:, 4 * n:4 * n + 4, :], src, ACT.Copy), t))
                    b.rd.append(ut[-1])
                b = bk[2]
                pe.wait(b.take())
                for h in range(4):
                    t = mm(b.t[:, h * 128:h * 128 + 128], kbg[:, 4 + h, :], TT[:, 4 + h, :], mark=h == 3)
                src = b.t[:, :].rearrange("p (a b) -> p a b", b=128)
                wt_ = act.do(act_(wT, src, ACT.Copy), t)
                b.rd.append(wt_)
                yield
                b = bk[3]
                pe.wait(b.take(), ut[0], *kg)
                for h in range(4):
                    t = mm(b.t[:, h * 128:h * 128 + 128], kT[:, h, :], U_[:, h, :], mark=h == 3)
                src = b.t[:, :].rearrange("p (a b) -> p a b", b=128)
                s1 = act.do(act_(S1, src, ACT.Copy), t)
                b.rd.append(s1)
                b = bk[0]
                pe.wait(b.take(), done["AT", 0])
                for h in range(4):
                    t = mm(b.t[:, h * 128:h * 128 + 128], U_[:, h, :], AT[:, h, :], mark=h == 3)
                o_ = cv[:, 8:12, :]
                src0 = b.t[:, :].rearrange("p (a b) -> p a b", b=128)
                o0 = act.do(act_(o_[:, :, 0:128], src0, ACT.Copy), t)
                b.rd.append(o0)
                yield
                b = bk[1]
                pe.wait(b.take(), s1, wt_)
                for h in range(4):
                    t = mm(b.t[:, h * 128:h * 128 + 128], wT[:, h, :], S1[:, h, :], mark=h == 3)
                src = b.t[:, :].rearrange("p (a b) -> p a b", b=128)
                vn = dve.do(tt_op(U_[:, 4:8, :], U_[:, 4:8, :], src, ALU.subtract), t, ut[1])
                b.rd.append(vn)
                yield
                b = bk[2]
                pe.wait(b.take(), vn, qd, done["AT", 1])
                for h in range(4):
                    o = b.t[:, h * 128:h * 128 + 128]
                    mm(o, S1[:, h, :], pre.rearrange("p a (b c) -> p (a b) c", c=128)[:, h, :], start=True, stop=False)
                    t = mm(o, U_[:, 4 + h, :], AT[:, 4 + h, :], start=False, stop=True, mark=h == 3)
                src = b.t[:, :].rearrange("p (a b) -> p a b", b=128)
                o1 = act.do(act_(o_[:, :, 128:256], src, ACT.Copy), t)
                b.rd.append(o1)
                yield
                sqo = [Y.rearrange("p (a b) c -> p a (b c)", b=2)[:, 2 * p:2 * p + 2, :] for p in range(2)]
                qt_ = [act.do(act_(sqo[p], o_[:, 2 * p:2 * p + 2, :], ACT.Square), o0, o1) for p in range(2)]
                dt = inv_diag(nr, 8, lambda i: sqo[i // 4][:, i // 2 % 2, (i % 2) * 128:(i % 2) * 128 + 128],
                              epsc[:, 0:1], 1.0 / 128, dia, qt_)
                zo = dve.do(ts_op(zf, zf, P(f"gng{l}"), None, ALU.mult), *zt)
                yield
                for p in range(2):
                    v = o_[:, 2 * p:2 * p + 2, :]
                    b = bk[p + 1]
                    pe.wait(b.take(), dt[p])
                    t = mm(b.t[:, :], ones, dia(4 * p).rearrange("p a b -> p (a b)"), mark=True)
                    src = b.t[:, :].rearrange("p (a b) -> p a b", b=256)
                    a = dve.do(tt_op(v, v, zf[:, 2 * p:2 * p + 2, :], ALU.mult), zo)
                    a = dve.do(tt_op(v, v, src, ALU.mult), t, a)
                    b.rd.append(a)
                    for k in (2 * p, 2 * p + 1):
                        oAt[k] = split(o_[:, k, :], h1[0][:, k, :], h1[1][:, k, :], waits=[a, done["brb"]])
                    yield
                done["A"] = 1

            side.append(delta())
            for i in range(4):
                b = banks[i % 2]
                t = gemm_fm(f"mw_z{l}", i, b, 0, xh, xl)
                a = act.do(act_(zf[:, i, :], b.t[:, 0:256], ACT.Silu, bias=P(f"bza{l}", i)), t)
                b.rd.append(a)
                zt.append(a)
                step()
            mt = {}

            def branch(br, oh, ot, waits_for):
                last = None
                for p in range(4):
                    bg, bo = banks[0], banks[1]
                    gemm_fm(f"mw_g{l}", br * 8 + 2 * p, bg, 0, xh, xl)
                    step()
                    t = gemm_fm(f"mw_g{l}", br * 8 + 2 * p + 1, bg, 1, xh, xl)
                    g = gt2[:, :, :]
                    gs = []
                    for i in range(2):
                        gs.append(act.do(act_(
                            g[:, i, :], bg.t[:, i * 256:i * 256 + 256], ACT.Sigmoid, bias=P(f"bg{l}", br * 8 + 2 * p + i)), t, mt.get("g")))
                    bg.rd.append(gs[-1])
                    step()
                    waits_for()
                    wv = ws.next(f"mw_br{l}", br * 4 + p)
                    pe.wait(bo.take())
                    for i in range(2):
                        o = bo.t[:, i * 256:i * 256 + 256]
                        for k in range(4):
                            pe.wait(*ot[k])
                            co = (i * 4 + k) * 128
                            t = mm3(o, wv[0][:, co:co + 128], wv[1][:, co:co + 128], oh[0][:, k, :], oh[1][:, k, :],
                                    k == 0, k == 3, None, i == 1 and k == 3)
                    ws.done(t)
                    last = t
                    m = mgs[p]
                    src = bo.t[:, :].rearrange("p (a b) -> p a b", b=256)
                    if br == 1:
                        a = dve.do(tt_op(m, g, src, ALU.mult), t, *gs)
                        bo.rd.append(a)
                        mt["g"] = a
                    else:
                        a = dve.do(tt_op(g, g, src, ALU.mult), t, *gs)
                        bo.rd.append(a)
                        a = dve.do(tt_op(m, m, g, ALU.add), a, mt[p])
                        mt["g"] = a
                    mt[p] = a
                    step()
                return last

            gt2 = R

            def until(key):
                def f():
                    while key not in done:
                        assert side
                        step()
                return f

            done["brb"] = branch(1, oB, oBt, until("B"))
            branch(2, oC, oCt, until("attn"))
            lastg = branch(0, h1, oAt, until("A"))
            finish()
            sp2 = []
            for k in range(8):
                sp2.append(split(mgs[k // 2][:, k % 2, :], xh[:, k, :], xl[:, k, :], waits=[mt[k // 2], lastg]))
            for k in range(8):
                toks = gemm_acc(f"mw_o{l}", k, xh, xl, k, k == 0, k == 7, waits=sp2[k])
            return toks

        phase = [0]

        def ended():
            phase[0] += 1
            return phase[0] >= stop

        def plain(toks):
            return [[add_pair(p, toks[p], 1.0)] for p in range(4)]

        def body(xt):
            toks = even(xt)
            if ended():
                return plain(toks)
            for i in range(2):
                if i:
                    toks = odd(toks)
                    if ended():
                        return plain(toks)
                pt, sq_, _ = rms_parts(f"nf{i}", toks)
                toks = ffn(f"fg{i}", f"fu{i}", f"fd{i}", 22, pt, stats=lambda: rms_stats(sq_, nxt=ACT.Silu))
                if ended():
                    return plain(toks)
            xs, _, _ = rms_parts(None, toks)
            for l in range(2):
                for f in range(2):
                    toks = ffn(f"sg{f}{l}", f"su{f}{l}", f"sd{f}{l}", 32, xs, half=0.5)
                    dve.wait(xready[0])
                    fin = l == 1 and f == 1
                    xs = layer_norm(f"l{2 * f + 1}g{l}", f"l{2 * f + 1}b{l}", toks, final=fin)
                    if fin:
                        return xs
                    if ended():
                        return xs + [[xready[0]]]
                    if f == 0:
                        toks = hybrid(l, xs)
                        dve.wait(xready[0])
                        xs = layer_norm(f"l2g{l}", f"l2b{l}", toks)
                        if ended():
                            return xs + [[xready[0]]]

        xt = body(xt)
        fr = everyone()
        otm = arena[:, 0:2048].rearrange("p (a b) -> p a b", b=1024)
        for hf in range(2):
            need = xt[4 * hf:4 * hf + 4] if len(xt) == 8 else xt
            for tt in range(2):
                b = banks[4 + tt * 2 + hf]
                pe.wait(b.take(), *[z for y in need for z in y])
                for k in range(4):
                    t = tr(b.t[:, k * 128:k * 128 + 128], x[:, hf * 4 + k, tt * 128:tt * 128 + 128], ident, mark=k == 3)
                dst = otm[:, tt, hf * 512:hf * 512 + 512]
                if tt:
                    a = act.do(act_(dst, b.t[:, :], ACT.Copy), t, fr)
                else:
                    a = dve.do(copy_op(dst, b.t[:, :]), t, fr)
                sp.dma(s_out, out[tt * 128:tt * 128 + 128, hf * 512:hf * 512 + 512], dst, a)
        sp.wait((s_out, s_out.n))
        if dry:
            return apos[0]

        block = ctx.enter_context(nc.Block())

        @block.sync
        def _(e):
            for f in sp.items:
                f(e)

        @block.scalar
        def _(e):
            for f in act.items:
                f(e)

        @block.vector
        def _(e):
            for f in dve.items:
                f(e)

        @block.gpsimd
        def _(e):
            for f in pool.items:
                f(e)

        @block.tensor
        def _(e):
            for f in pe.items:
                f(e)
        return apos[0]


def fm(w):
    K, N = w.shape
    return w.reshape(K // 128, 128, N // 128, 128).transpose(2, 1, 0, 3).reshape(N // 128, 128, K)


def tm(w, kper, n):
    K, N = w.shape
    return w.reshape(K // (kper * 128), kper, 128, N // n, n).transpose(3, 0, 2, 1, 4).reshape(-1, 128, kper * n)


def cols(v):
    return v.reshape(-1, 128).T


def lay_out(a):
    d = {}
    w = a["even_w_in"][0]
    d["ew_c"] = fm(w[:, 1024:1664])
    d["ew_pe"] = tm(w[:, 1664:1696], 8, 32)
    d["ew_u"] = fm(w[:, 0:512])
    d["ew_v"] = tm(w[:, 512:1024], 2, 512)
    d["ew_ukv"] = tm(a["mla_w_ukv"][0], 2, 512)
    d["ew_uq"] = tm(a["mla_w_uq"][0], 1, 384)
    d["ew_out"] = a["even_w_out"][0].reshape(8, 128, 1024)
    w = a["odd_w_in"][0]
    d["ow_v"] = tm(w[:, 2048:4096], 2, 512)
    qk = fm(w[:, 0:2048]).reshape(2, 4, 2, 128, 1024)
    d["ow_qk"] = qk.transpose(1, 0, 2, 3, 4).reshape(16, 128, 1024)
    d["ow_g"] = fm(w[:, 4096:6144])
    d["ow_out"] = a["odd_w_out"][0].reshape(16, 128, 1024)
    for i in range(2):
        d[f"fg{i}"] = fm(a["ffn_w_gate"][i])
        d[f"fu{i}"] = fm(a["ffn_w_up"][i])
        d[f"fd{i}"] = a["ffn_w_down"][i].reshape(22, 128, 1024)
    pk = [cols(a["norm_mix"][0]), cols(a["norm_mix"][1]), cols(a["norm_ffn"][0]), cols(a["norm_ffn"][1]),
          cols(a["gm_v_norm"][0]), cols(a["mla_q_a_norm"][0]), cols(a["mla_kv_a_norm"][0]), cols(a["ret_out_norm"][0])]
    qperm = np.concatenate([np.r_[j * 64:j * 64 + 64, (4 + j) * 64:(4 + j) * 64 + 64] for j in range(4)])
    hperm = [0, 4, 1, 5, 2, 6, 3, 7]
    own = np.arange(128)[None, :] // 64 <= np.arange(128)[:, None] // 64
    for l in range(2):
        for f in range(2):
            w = a[f"w_ff{f + 1}_in_2"][l]
            d[f"sg{f}{l}"] = fm(w[:, 0:4096])
            d[f"su{f}{l}"] = fm(w[:, 4096:8192])
            d[f"sd{f}{l}"] = a[f"w_ff{f + 1}_out_2"][l].reshape(32, 128, 1024)
        w, b = a["w_in_2"][l], a["b_in_2"][l]
        d[f"mw_qkb{l}"] = fm(w[:, 2056:3080])
        d[f"mw_vb{l}"] = tm(w[:, 3080:3592], 2, 512)
        qc = w[:, 3592:4104][:, qperm]
        d[f"mw_c{l}"] = np.concatenate([fm(np.concatenate([qc, w[:, 4104:4232]], 1)), tm(w[:, 4232:4360], 8, 128)])
        d[f"mw_ba{l}"] = tm(w[:, 1536:1544], 8, 8)
        d[f"mw_a{l}"] = fm(w[:, 0:1536])
        d[f"mw_z{l}"] = fm(w[:, 1544:2056])
        d[f"mw_g{l}"] = fm(a["w_gate_2"][l])
        brs = [a["w_br_a_2"][l], a["w_br_b_2"][l], a["w_br_c_2"][l][qperm]]
        d[f"mw_br{l}"] = np.concatenate(
            [v.reshape(4, 128, 4, 2, 128).transpose(2, 1, 3, 0, 4).reshape(4, 128, 1024) for v in brs])
        d[f"mw_o{l}"] = a["w_out_2"][l].reshape(8, 128, 1024)
        d[f"rowc{l}"] = np.concatenate([b[3080:3592], b[4232:4360], b[1536:1544], a["a_log_2"][l], a["dt_bias_2"][l],
                                        a["sinks_2"][l][hperm]])
        q, m = np.arange(128)[:, None], np.arange(256)[None, :]
        idx = np.clip(128 + q - m, -63, 128) + 63
        rb = a["rel_bias_2"][l][:, idx]
        rb[:, :, 128:] = np.where(own[None], rb[:, :, 128:], np.float32(NEG))
        d[f"relb{l}"] = np.concatenate([rb[:, :, 128:], rb], 2).transpose(1, 0, 2)
        pk += [cols(a[n][l]) for n in ("ln1_g_2", "ln1_b_2", "ln2_g_2", "ln2_b_2", "ln3_g_2", "ln3_b_2")]
        pk += [cols(b[0:1536]), cols(b[1544:2056]), cols(b[2056:2568]), cols(b[2568:3080]), cols(b[3592:4104][qperm]),
               cols(b[4104:4232]), cols(a["b_gate_2"][l]), cols(a["conv_w_2"][l]), cols(a["gdn_norm_g_2"][l])]
    d["pack"] = np.concatenate(pk, 1)
    d["rowa"] = np.concatenate([a["mla_q_norm"][0], a["mla_k_norm"][0], a["gm_b_s"][0].reshape(-1)])
    d["gmw"] = a["gm_w_s"][0]
    d["x"] = a["x"][0]
    return d


def constants():
    f = np.float32
    i = np.arange(128)
    c = {"ident": np.eye(128), "ones": np.ones((128, 128)), "U": i[:, None] <= i[None, :],
         "nSU": -(i[:, None] < i[None, :]).astype(f), "NEGU": np.where(i[:, None] <= i[None, :], 0.0, NEG)}
    own = np.where(i[None, :] // 64 <= i[:, None] // 64, 0.0, NEG)
    c["mask"] = np.concatenate([own, np.zeros((128, 128)), own], 1)
    dist = 128 + i[:, None] - np.arange(256)[None, :]
    qch, kch = 2 + i[:, None] // 64, np.arange(256)[None, :] // 64
    nd = np.where((kch <= qch) & (kch >= qch - 2), -np.abs(dist), NEG)
    c["negd"] = np.concatenate([nd[:, 128:], nd], 1)
    inv = (f(10000.0) ** (-np.arange(128, dtype=f) / f(128))).astype(f)
    ang = (np.arange(256, dtype=f)[None, :] * inv[:, None]).astype(f)
    co, si = np.cos(ang), np.sin(ang)
    c["cc"] = np.concatenate([co, co], 1)
    c["ss"] = np.concatenate([-si, si], 1)
    lg = np.log(1.0 - 2.0 ** (-5.0 - np.arange(4)))
    dd = np.arange(256)[None, None, :] - i[:, None, None]
    c["dtr"] = np.where(dd >= 0, np.exp(lg[None, :, None] * np.maximum(dd, 0)), 0.0).reshape(128, 1024)
    inv = (f(10000.0) ** (-np.arange(16, dtype=f) / f(16))).astype(f)
    ang = (np.arange(256, dtype=f)[:, None] * inv[None, :]).astype(f).reshape(2, 128, 16).transpose(1, 0, 2).reshape(128, 32)
    c["cosT"], c["sinT"] = np.cos(ang), np.sin(ang)
    out = np.concatenate([np.asarray(c[n], f).reshape(128, w) for n, w in CONSTS], 1)
    lv = np.zeros((128, 14, 128), f)
    for k in range(7):
        bi, bj = i[:, None] >> k, i[None, :] >> k
        m = (bi % 2 == 1) & (bj == bi - 1)
        lv[:, k, :] = m
        lv[:, 7 + k, :] = m.T
    return out, lv


STOP = 99


def kernel(**inputs):
    import concourse.bacc as _bacc
    from concourse import mybir as _mybir
    from concourse.bass_utils import run_bass_kernel_spmd as _run

    a = {k: np.asarray(v) for k, v in inputs.items()}
    arrays = lay_out(a)
    arrays["consts"], arrays["lvmask"] = constants()
    arrays = {f"in_{k}": np.ascontiguousarray(v) for k, v in arrays.items()}

    def build(order, dry):
        nc = _bacc.Bacc("TRN2", target_bir_lowering=False, num_devices=1)
        ins = {k[3:]: nc.dram_tensor(k, v.shape, _mybir.dt.from_np(v.dtype), kind="ExternalInput").ap()
               for k, v in arrays.items()}
        out = nc.dram_tensor("out_0_dram", (256, 1024), F32, kind="ExternalOutput").ap()
        emit(nc, ins, out, STOP, order, dry)
        return nc

    order = []
    build(order, True)
    nc = build(order, False)
    r = _run(nc, [arrays], core_ids=[0])
    return r.results[0]["out_0_dram"].reshape(1, 256, 1024)
```
